# Optimizing a Trainium2 kernel written in Bass

```python
import jax
import jax.numpy as jnp
from jax import lax
import numpy as np

D_MODEL = 2048
BATCH = 1
SEQ = 256
DEPTH = 2

MIX_WIDTH = D_MODEL
RET_WIDTH = D_MODEL // 4
RET_HEAD_DIM = 128
RET_HEADS = RET_WIDTH // RET_HEAD_DIM
RET_CHUNK = 128
RWKV_WIDTH = D_MODEL // 4
RWKV_HEAD_DIM = 64
RWKV_HEADS = RWKV_WIDTH // RWKV_HEAD_DIM
RWKV_DECAY_RANK = max(32, int(round(1.8 * D_MODEL ** 0.5 / 32)) * 32)
RWKV_A_RANK = max(32, int(round(1.8 * D_MODEL ** 0.5 / 32)) * 32)
RWKV_V_RANK = max(32, int(round(1.3 * D_MODEL ** 0.5 / 32)) * 32)
RWKV_GATE_RANK = max(32, int(round(0.6 * D_MODEL ** 0.8 / 32)) * 32)
RWKV_GN_EPS = 64e-5
NSA_WIDTH = MIX_WIDTH - RET_WIDTH - RWKV_WIDTH
NSA_HEAD_DIM = 64
NSA_HEADS = NSA_WIDTH // NSA_HEAD_DIM
NSA_KV_GROUPS = 4
NSA_KV_WIDTH = NSA_KV_GROUPS * NSA_HEAD_DIM
CMP_BLOCK = 32
CMP_STRIDE = 16
CMP_HIDDEN = 4 * NSA_HEAD_DIM
SLC_BLOCK = 64
SLC_TOPK = 16
WINDOW = 512
Q_BLOCK = 128
ROPE_THETA = 10000.0
MLP_HIDDEN = 4 * D_MODEL
RMS_EPS = 1e-6
NEG_INF = -1e30
FORCED_SCORE = 1e9

RET_IN_SIZES = (RET_WIDTH,) * 4
RWKV_IN_SIZES = (RWKV_WIDTH,) * 3 + (RWKV_DECAY_RANK, RWKV_A_RANK, RWKV_GATE_RANK)
NSA_IN_SIZES = (NSA_WIDTH,) + (NSA_KV_WIDTH,) * 6 + (3 * NSA_HEADS,)
RET_IN = sum(RET_IN_SIZES)
RWKV_IN = sum(RWKV_IN_SIZES)
NSA_IN = sum(NSA_IN_SIZES)
IN_WIDTH = RET_IN + RWKV_IN + NSA_IN

kernel_name = 'hybrid_retention_rwkv7_nsa_block'

def _split(a, sizes):
    return jnp.split(a, np.cumsum(np.array(sizes))[:-1].tolist(), axis=-1)

def _rms_norm(x, gain=None, eps=RMS_EPS):
    xf = x.astype(jnp.float32)
    y = xf * lax.rsqrt(jnp.mean(xf * xf, axis=-1, keepdims=True) + eps)
    if gain is not None:
        y = y * gain.astype(jnp.float32)
    return y.astype(x.dtype)

def _rope(x, pos):
    half = x.shape[-1] // 2
    inv_freq = ROPE_THETA ** (-jnp.arange(half, dtype=jnp.float32) / half)
    ang = pos.astype(jnp.float32)[:, None] * inv_freq[None, :]
    cos = jnp.cos(ang)[None, :, None, :]
    sin = jnp.sin(ang)[None, :, None, :]
    xf = x.astype(jnp.float32)
    x1, x2 = xf[..., :half], xf[..., half:]
    return jnp.concatenate([x1 * cos - x2 * sin, x1 * sin + x2 * cos], axis=-1).astype(x.dtype)

def _token_shift(p):
    return jnp.pad(p, ((0, 0), (1, 0), (0, 0)))[:, :-1]

def _retention(q, k, v, gate):
    B, T, _ = q.shape
    H, Dh, C = RET_HEADS, RET_HEAD_DIM, RET_CHUNK
    n_chunks = T // C
    pos = jnp.arange(T)
    qf = _rope(q.reshape(B, T, H, Dh), pos).astype(jnp.float32)
    kf = _rope(k.reshape(B, T, H, Dh), pos).astype(jnp.float32) * Dh ** -0.5
    vf = v.reshape(B, T, H, Dh).astype(jnp.float32)
    log_gamma = jnp.log(1.0 - 2.0 ** (-5.0 - jnp.arange(H, dtype=jnp.float32)))
    n = jnp.arange(C, dtype=jnp.float32)
    lag = n[:, None] - n[None, :]
    decay_mat = jnp.where(lag >= 0, jnp.exp(jnp.maximum(lag, 0.0)[None] * log_gamma[:, None, None]), 0.0)
    q_decay = jnp.exp((n + 1.0)[None, :] * log_gamma[:, None])[None, :, :, None]
    k_decay = jnp.exp((C - 1.0 - n)[None, :] * log_gamma[:, None])[None, :, :, None]
    chunk_decay = jnp.exp(C * log_gamma)[None, :, None, None]

    def to_chunks(a):
        return a.reshape(B, n_chunks, C, H, Dh).transpose(1, 0, 3, 2, 4)

    def chunk_step(state, inp):
        qc, kc, vc = inp
        inner = jnp.einsum('bhnd,bhmd->bhnm', qc, kc) * decay_mat[None]
        out = jnp.einsum('bhnm,bhmd->bhnd', inner, vc) + jnp.einsum('bhnd,bhde->bhne', qc, state) * q_decay
        state = chunk_decay * state + jnp.einsum('bhmd,bhme->bhde', kc * k_decay, vc)
        return state, out

    state0 = jnp.zeros((B, H, Dh, Dh), jnp.float32)
    _, out = lax.scan(chunk_step, state0, (to_chunks(qf), to_chunks(kf), to_chunks(vf)))
    out = out.transpose(1, 0, 3, 2, 4).reshape(B, T, H, Dh)
    out = _rms_norm(out).reshape(B, T, H * Dh)
    return (jax.nn.silu(gate.astype(jnp.float32)) * out).astype(q.dtype)

def _wkv7(r, w, k, v, a, b):
    def step(S, inp):
        r_t, w_t, k_t, v_t, a_t, b_t = inp
        sa = jnp.einsum('bhij,bhj->bhi', S, a_t)
        S = S * w_t[:, :, None, :] + sa[..., :, None] * b_t[..., None, :] + v_t[..., :, None] * k_t[..., None, :]
        return S, jnp.einsum('bhij,bhj->bhi', S, r_t)

    B, T, H, N = r.shape
    seq_major = tuple(t.transpose(1, 0, 2, 3) for t in (r, w, k, v, a, b))
    _, y = lax.scan(step, jnp.zeros((B, H, N, N), jnp.float32), seq_major)
    return y.transpose(1, 0, 2, 3)

def _rwkv7(p, vres_p, v_first, mix, vres_mix, w0, w2, a0, a2, v0, v2, g2, k_k, k_a, r_k, ln_g, ln_b):
    B, T, _ = p.shape
    H, N = RWKV_HEADS, RWKV_HEAD_DIM
    f32 = jnp.float32
    dt = p.dtype
    p = (p + mix * (_token_shift(p) - p)).astype(f32)
    r, k, v, xw, xa, xg = _split(p, RWKV_IN_SIZES)
    w = -jax.nn.softplus(-(w0 + jnp.tanh(xw) @ w2)) - 0.5
    decay = jnp.exp(-jnp.exp(w))
    if vres_p is None:
        v_first = v
    else:
        xv = (vres_p + vres_mix * (_token_shift(vres_p) - vres_p)).astype(f32)
        v = v + (v_first - v) * jax.nn.sigmoid(v0 + xv @ v2)
    a = jax.nn.sigmoid(a0 + xa @ a2)
    g = jax.nn.sigmoid(xg) @ g2
    kk = (k * k_k).reshape(B, T, H, N)
    kk = kk / jnp.maximum(jnp.sqrt(jnp.sum(kk * kk, axis=-1, keepdims=True)), 1e-12)
    k = k * (1.0 + (a - 1.0) * k_a)
    rh = r.reshape(B, T, H, N)
    kh = k.reshape(B, T, H, N)
    vh = v.reshape(B, T, H, N)
    ah = a.reshape(B, T, H, N)
    y = _wkv7(rh, decay.reshape(B, T, H, N), kh, vh, -kk, kk * ah)
    mu = jnp.mean(y, axis=-1, keepdims=True)
    var = jnp.mean(jnp.square(y - mu), axis=-1, keepdims=True)
    y = (y - mu) * lax.rsqrt(var + RWKV_GN_EPS) * ln_g.reshape(H, N) + ln_b.reshape(H, N)
    y = y + jnp.sum(rh * kh * r_k, axis=-1, keepdims=True) * vh
    return (y.reshape(B, T, H * N) * g).astype(dt), v_first

def _nsa(q, kc, vc, ks, vs, kw, vw, gate_logits, q_norm, k_norm, cmp_pe, cmp_k_w1, cmp_k_w2, cmp_v_w1, cmp_v_w2):
    B, T, _ = q.shape
    H, G, Dh = NSA_HEADS, NSA_KV_GROUPS, NSA_HEAD_DIM
    Hg = H // G
    f32 = jnp.float32
    n_q_blocks = T // Q_BLOCK
    n_cmp = (T - CMP_BLOCK) // CMP_STRIDE + 1
    n_slc = T // SLC_BLOCK
    n_sel = min(SLC_TOPK, n_slc)
    pos = jnp.arange(T)

    def kv(t):
        return t.reshape(B, T, G, Dh)

    q = _rope(_rms_norm(q.reshape(B, T, H, Dh), q_norm), pos) * Dh ** -0.5

    cmp_start = jnp.arange(n_cmp) * CMP_STRIDE
    cmp_end = cmp_start + CMP_BLOCK - 1
    gather_ix = cmp_start[:, None] + jnp.arange(CMP_BLOCK)[None, :]

    def compress(t, pe, w1, w2):
        blocks = kv(t)[:, gather_ix] + pe[None, None, :, None, :]
        blocks = blocks.transpose(0, 1, 3, 2, 4).reshape(B, n_cmp, G, CMP_BLOCK * Dh)
        return jax.nn.gelu(blocks @ w1) @ w2

    k_cmp = _rope(_rms_norm(compress(kc, cmp_pe[0], cmp_k_w1, cmp_k_w2), k_norm[0]), cmp_end)
    v_cmp = compress(vc, cmp_pe[1], cmp_v_w1, cmp_v_w2)

    slc_start = jnp.arange(n_slc) * SLC_BLOCK
    cmp_in_slc = ((cmp_start[:, None] <= slc_start[None, :] + SLC_BLOCK - 1)
                  & (cmp_end[:, None] >= slc_start[None, :])).astype(f32)

    def blockify(t):
        return t.reshape(B, n_slc, SLC_BLOCK, G, Dh).transpose(0, 3, 1, 2, 4)

    k_slc = blockify(_rope(_rms_norm(kv(ks), k_norm[1]), pos))
    v_slc = blockify(kv(vs))

    pad = ((0, 0), (WINDOW, 0), (0, 0), (0, 0))
    k_win = jnp.pad(_rope(_rms_norm(kv(kw), k_norm[2]), pos), pad)
    v_win = jnp.pad(kv(vw), pad)

    b_ix = jnp.arange(B)[:, None, None, None]
    g_ix = jnp.arange(G)[None, None, :, None]
    blk_ids = jnp.arange(n_slc)[None, :]

    def masked_softmax(s, visible):
        return jax.nn.softmax(jnp.where(visible, s.astype(f32), NEG_INF), axis=-1)

    def query_block(args):
        qb, gb, qi = args
        t = qi * Q_BLOCK + jnp.arange(Q_BLOCK)
        vis_c = (cmp_end[None, :] <= t[:, None])[None, :, None, None, :]
        p_c = masked_softmax(jnp.einsum('bqghd,bngd->bqghn', qb, k_cmp), vis_c) * vis_c
        o_c = jnp.einsum('bqghn,bngd->bqghd', p_c.astype(v_cmp.dtype), v_cmp)
        score = jnp.einsum('bqghn,ns->bqgs', p_c, cmp_in_slc)
        cur = (t // SLC_BLOCK)[:, None]
        forced = (blk_ids == 0) | (blk_ids == cur) | (blk_ids == cur - 1)
        score = jnp.where(forced[None, :, None, :], FORCED_SCORE, score)
        score = jnp.where((blk_ids <= cur)[None, :, None, :], score, -jnp.inf)
        _, sel = lax.top_k(score, n_sel)
        k_sel = k_slc[b_ix, g_ix, sel]
        v_sel = v_slc[b_ix, g_ix, sel]
        tok = sel[..., None] * SLC_BLOCK + jnp.arange(SLC_BLOCK)
        vis_s = (tok <= t[None, :, None, None, None]).reshape(B, Q_BLOCK, G, 1, n_sel * SLC_BLOCK)
        s_s = jnp.einsum('bqghd,bqgnkd->bqghnk', qb, k_sel)
        p_s = masked_softmax(s_s.reshape(B, Q_BLOCK, G, Hg, n_sel * SLC_BLOCK), vis_s)
        o_s = jnp.einsum('bqghnk,bqgnkd->bqghd', p_s.reshape(s_s.shape).astype(v_sel.dtype), v_sel)
        start = qi * Q_BLOCK
        k_w = lax.dynamic_slice_in_dim(k_win, start, Q_BLOCK + WINDOW, axis=1)
        v_w = lax.dynamic_slice_in_dim(v_win, start, Q_BLOCK + WINDOW, axis=1)
        kpos = start - WINDOW + jnp.arange(Q_BLOCK + WINDOW)
        lag = t[:, None] - kpos[None, :]
        vis_w = ((lag >= 0) & (lag < WINDOW) & (kpos[None, :] >= 0))[None, :, None, None, :]
        p_w = masked_softmax(jnp.einsum('bqghd,bkgd->bqghk', qb, k_w), vis_w)
        o_w = jnp.einsum('bqghk,bkgd->bqghd', p_w.astype(v_w.dtype), v_w)
        gate = jax.nn.sigmoid(gb.astype(f32))
        out = gate[..., 0:1] * o_c + gate[..., 1:2] * o_s + gate[..., 2:3] * o_w
        return out.astype(qb.dtype)

    q_blocks = q.reshape(B, n_q_blocks, Q_BLOCK, G, Hg, Dh).transpose(1, 0, 2, 3, 4, 5)
    g_blocks = gate_logits.reshape(B, n_q_blocks, Q_BLOCK, G, Hg, 3).transpose(1, 0, 2, 3, 4, 5)
    out = lax.map(query_block, (q_blocks, g_blocks, jnp.arange(n_q_blocks)))
    return out.transpose(1, 0, 2, 3, 4, 5).reshape(B, T, NSA_WIDTH)

def setup_inputs(seed: int = 0) -> dict:
    key = jax.random.key(seed)
    keys = iter(jax.random.split(key, 40))

    def nrm(shape, scale):
        return jax.random.normal(next(keys), shape, jnp.float32) * scale

    def uni(shape, lo, hi):
        return jax.random.uniform(next(keys), shape, jnp.float32, lo, hi)

    L, Lv = DEPTH, DEPTH - 1
    RW, H, N, Dh = RWKV_WIDTH, RWKV_HEADS, RWKV_HEAD_DIM, NSA_HEAD_DIM
    return {
        'x': nrm((BATCH, SEQ, D_MODEL), 1.0),
        'ln1_g': 1.0 + nrm((L, D_MODEL), 0.02),
        'w_in': nrm((L, D_MODEL, IN_WIDTH), D_MODEL ** -0.5),
        'w_in_vres': nrm((Lv, D_MODEL, RWKV_V_RANK), D_MODEL ** -0.5),
        'rwkv_mix': uni((L, RWKV_IN), 0.0, 1.0),
        'rwkv_vres_mix': uni((Lv, RWKV_V_RANK), 0.0, 1.0),
        'rwkv_w0': uni((L, RW), -6.0, -1.0),
        'rwkv_w2': nrm((L, RWKV_DECAY_RANK, RW), RWKV_DECAY_RANK ** -0.5),
        'rwkv_a0': nrm((L, RW), 0.01),
        'rwkv_a2': nrm((L, RWKV_A_RANK, RW), RWKV_A_RANK ** -0.5),
        'rwkv_v0': 1.0 + nrm((Lv, RW), 0.1),
        'rwkv_v2': nrm((Lv, RWKV_V_RANK, RW), RWKV_V_RANK ** -0.5),
        'rwkv_g2': nrm((L, RWKV_GATE_RANK, RW), RWKV_GATE_RANK ** -0.5),
        'rwkv_k_k': 0.85 + nrm((L, RW), 0.02),
        'rwkv_k_a': 1.0 + nrm((L, RW), 0.02),
        'rwkv_r_k': nrm((L, H, N), 0.1),
        'rwkv_ln_g': 1.0 + nrm((L, RW), 0.02),
        'rwkv_ln_b': nrm((L, RW), 0.01),
        'nsa_q_norm': 1.0 + nrm((L, Dh), 0.02),
        'nsa_k_norm': 1.0 + nrm((L, 3, Dh), 0.02),
        'nsa_cmp_pe': nrm((L, 2, CMP_BLOCK, Dh), 0.02),
        'nsa_cmp_k_w1': nrm((L, CMP_BLOCK * Dh, CMP_HIDDEN), (CMP_BLOCK * Dh) ** -0.5),
        'nsa_cmp_k_w2': nrm((L, CMP_HIDDEN, Dh), CMP_HIDDEN ** -0.5),
        'nsa_cmp_v_w1': nrm((L, CMP_BLOCK * Dh, CMP_HIDDEN), (CMP_BLOCK * Dh) ** -0.5),
        'nsa_cmp_v_w2': nrm((L, CMP_HIDDEN, Dh), CMP_HIDDEN ** -0.5),
        'w_out': nrm((L, MIX_WIDTH, D_MODEL), MIX_WIDTH ** -0.5),
        'ln2_g': 1.0 + nrm((L, D_MODEL), 0.02),
        'w_up': nrm((L, D_MODEL, MLP_HIDDEN), D_MODEL ** -0.5),
        'w_down': nrm((L, MLP_HIDDEN, D_MODEL), MLP_HIDDEN ** -0.5),
    }

def reference(x, ln1_g, w_in, w_in_vres, rwkv_mix, rwkv_vres_mix, rwkv_w0, rwkv_w2, rwkv_a0, rwkv_a2,
              rwkv_v0, rwkv_v2, rwkv_g2, rwkv_k_k, rwkv_k_a, rwkv_r_k, rwkv_ln_g, rwkv_ln_b,
              nsa_q_norm, nsa_k_norm, nsa_cmp_pe, nsa_cmp_k_w1, nsa_cmp_k_w2, nsa_cmp_v_w1, nsa_cmp_v_w2,
              w_out, ln2_g, w_up, w_down):
    v_first = None
    for l in range(DEPTH):
        h = _rms_norm(x, ln1_g[l])
        if l == 0:
            w_l = w_in[l]
            group_sizes = (RET_IN, RWKV_IN, NSA_IN)
            vres_mix, v0, v2 = None, None, None
        else:
            w_l = jnp.concatenate([w_in[l], w_in_vres[l - 1]], axis=1)
            group_sizes = (RET_IN, RWKV_IN, NSA_IN, RWKV_V_RANK)
            vres_mix, v0, v2 = rwkv_vres_mix[l - 1], rwkv_v0[l - 1], rwkv_v2[l - 1]
        proj = jnp.einsum('btd,dn->btn', h, w_l)
        parts = _split(proj, group_sizes)
        vres_p = parts[3] if l > 0 else None
        o_ret = _retention(*_split(parts[0], RET_IN_SIZES))
        o_rwkv, v_first = _rwkv7(parts[1], vres_p, v_first, rwkv_mix[l], vres_mix, rwkv_w0[l], rwkv_w2[l],
                                 rwkv_a0[l], rwkv_a2[l], v0, v2, rwkv_g2[l], rwkv_k_k[l], rwkv_k_a[l],
                                 rwkv_r_k[l], rwkv_ln_g[l], rwkv_ln_b[l])
        o_nsa = _nsa(*_split(parts[2], NSA_IN_SIZES), nsa_q_norm[l], nsa_k_norm[l], nsa_cmp_pe[l],
                     nsa_cmp_k_w1[l], nsa_cmp_k_w2[l], nsa_cmp_v_w1[l], nsa_cmp_v_w2[l])
        mixed = jnp.concatenate([o_ret, o_rwkv, o_nsa], axis=-1)
        x = x + jnp.einsum('btm,md->btd', mixed, w_out[l])
        h = _rms_norm(x, ln2_g[l])
        up = jnp.square(jax.nn.relu(jnp.einsum('btd,df->btf', h, w_up[l])))
        x = x + jnp.einsum('btf,fd->btd', up, w_down[l])
    return x


_drawn_inputs = setup_inputs


def setup_inputs(seed=0):
    import zlib

    import numpy as np

    out = dict(_drawn_inputs(seed))
    spreads = {}
    factors = {'rwkv_w2': 2.701,
     'rwkv_a0': 8.0,
     'rwkv_v0': 64.0,
     'rwkv_k_k': 8.0,
     'rwkv_k_a': 7.087,
     'rwkv_ln_g': 8.0,
     'rwkv_ln_b': 26.264,
     'nsa_q_norm': 8.0,
     'nsa_k_norm': 8.0,
     'nsa_cmp_pe': 8.0,
     'w_in_vres': 8.0,
     'rwkv_vres_mix': 8.0,
     'rwkv_v2': 8.0}
    for name, (base, spread) in spreads.items():
        noise = np.random.default_rng([zlib.crc32(name.encode()), seed]).standard_normal(out[name].shape)
        drawn = base * np.exp(spread * noise) if base else spread * noise
        out[name] = jnp.asarray(drawn.astype(out[name].dtype))
    for name, factor in factors.items():
        out[name] = (out[name] * factor).astype(out[name].dtype)
    return out
```

```python
import concourse.bass as bass
from concourse import mybir
from contextlib import ExitStack

D, T, DEPTH = 2048, 256, 2
KT = D // 128
N_IN, N_CMP, N_OUT, N_GRP = 53, 4, 16, 4
LAYER_SLABS = N_IN + N_CMP + N_OUT + N_GRP * 32
SLABS = DEPTH * LAYER_SLABS
RING = 4
HALF = KT // 2
RW_R, RW_K, RW_V, RW_W, RW_A, RW_G, RW_X = 0, 4, 8, 12, 13, 14, 16
RT_Q, RT_K, RT_V, RT_G = 17, 21, 25, 29
NS_Q, NS_KS, NS_KW, NS_KC, NS_VC, NS_VS, NS_VW = 33, 41, 43, 45, 47, 49, 51
M_RW, M_RT, M_NS = 0, 4, 8
VEC = {}
_at = 0
for _n, _w in [("g1", 16), ("g2", 16), ("mix", 17), ("w0", 4), ("a0", 4), ("v0", 4), ("kk", 4), ("ka", 4), ("rk", 4),
               ("lng", 4), ("lnb", 4), ("qn", 1), ("kn_c", 1), ("kn_s", 1), ("kn_w", 1), ("pe_k", 16), ("pe_v", 16)]:
    VEC[_n] = (_at, _at + _w)
    _at += _w
NVEC = _at
CON = {}
_at = 0
for _n, _w in [("ident", 128), ("one_d", 128), ("blk_mean", 128), ("blk_sum", 128), ("one_h", 128), ("rot_r", 128),
               ("rot_n", 128), ("cos_r", 256), ("sin_r", 256), ("cos_n", 256), ("sin_n", 256), ("cos_c", 16), ("sin_c", 16),
               ("decay", 1024), ("causal", 256), ("cmp_add", 32), ("cmp_vis", 32), ("rw_mask", 256), ("lev", 768),
               ("scan", 256), ("vcz", 8)]:
    CON[_n] = (_at, _at + _w)
    _at += _w
NCON = _at
LW = {"w2": (0, 512), "a2": (512, 1024), "v2": (1024, 1536), "g2": (1536, 2560)}
NLW = 2560
CW = {"k2": (0, 256), "v2": (256, 384)}
NCW = 384
KAPPA = 0.6065306597126334


def hybrid_trunk(nc, slabs, x_in, vecs, consts, small, cmpw, out, v_first, dbg=None):
    f32, f32r = mybir.dt.float32, mybir.dt.float32r
    ACT, ALU, AX = mybir.ActivationFunctionType, mybir.AluOpType, mybir.AxisListType
    ctx = ExitStack()
    with ctx:
        base = [16640]

        def place(name, cols, dt=f32, at=None):
            if at is None:
                at, base[0] = base[0], base[0] + (4 * cols + 31) // 32 * 32
            return nc.alloc_sbuf_tensor_at(name, [128, cols], dt, offset=at)

        X_t = place("x_res", KT * T)
        F0B = base[0]
        F0_t = place("act_f0", KT * 2 * T, f32r)
        RA = nc.alloc_sbuf_tensor_at("scratch_a", [128, 8192], f32, offset=F0B)
        BLK_t = nc.alloc_sbuf_tensor_at("cmp_blocks", [128, 2 * 16 * 120], f32r, offset=F0B)
        PB = base[0]
        P_t = place("proj", N_IN * T)
        F1_t = place("act_f1", KT * 2 * T, f32r, PB)
        U_t = place("act_up", KT * 2 * T, f32r, PB + 32768)
        LW_t = place("lowrank_w", NLW, at=PB + N_IN * T * 4)
        base[0] = PB + 65536
        raw_t = place("raw", RING * KT * 128)
        RBB = base[0]
        hi_t = place("w_hi", 4 * HALF * 128, f32r)
        lo_t = place("w_lo", 4 * HALF * 128, f32r)
        RB = nc.alloc_sbuf_tensor_at("scratch_b", [128, 8192], f32, offset=RBB)
        bc_t = place("bcopy", 2 * T)
        s_t = place("evac_s", T)
        t_t = place("evac_t", T)
        sq_t = place("evac_sq", T)
        rstd_t = place("rstd", T)
        acc_t = place("sumsq", T)
        psq_t = place("psq", T)
        CM_t = place("consts_sb", NCON)
        VV_t = place("vecs_sb", DEPTH * NVEC)
        CW_t = place("cmp_w2", NCW)
        ST_t = place("state", 256)
        SN_t = place("state_new", 256)
        WC_t = place("chunk_decay", 16)
        EPS_t = place("eps", 8)
        KTC_t = place("k_cmp", 64)
        assert base[0] <= 229368, base[0]

        P = P_t[:, :].rearrange("p (k t) -> p k t", t=T)

        def con(name):
            return CM_t[:, CON[name][0]:CON[name][1]]

        def vec(l, name, i=0):
            c = l * NVEC + VEC[name][0] + i
            return VV_t[:, c:c + 1]

        def eps(i):
            return EPS_t[:, i:i + 1]
        E_RMS, E_KK, E_LN8, E_GN = 0, 1, 2, 3

        PS_t = ctx.enter_context(nc.psum_tensor("banks", [128, 8, 512], f32))
        HID = P_t[:, NS_KC * T:(NS_KC + 4) * T]
        PD = P_t[:, RT_Q * T:]
        VF_t = PD[:, 7168:8192]
        BD, TA, TB, PP, NM = RB[:, 4096:6144], RB[:, 0:1024], RB[:, 2048:3072], RB[:, 6144:7168], RB[:, 7168:8192]
        LBK = PD[:, 2048:6144]
        LB, LK = LBK[:, 0:2048], LBK[:, 2048:4096]
        UN = [(qt, tt, br) for qt in range(8) for tt in range(2) for br in range(2)]

        def bankc(j, w):
            return PS_t[:, j, 0:w]

        sems = {}

        def sem(name):
            if name not in sems:
                sems[name] = ctx.enter_context(nc.semaphore(name))
            return sems[name]

        raw_in = [sem(f"raw_in{i}") for i in range(RING)]
        x_in_s, con_in, vec_in = sem("x_in"), sem("con_in"), sem("vec_in")
        hi_ready, lo_ready, half_done = sem("hi_ready"), sem("lo_ready"), sem("half_done")
        bc_ready, sum_ready, evac_done = sem("bc_ready"), sem("sum_ready"), sem("evac_done")
        up_scaled, up_sq, u_hi = sem("up_scaled"), sem("up_sq"), sem("u_hi")
        x_upd, x_hi, x_lo, xg_ready = sem("x_upd"), sem("x_hi"), sem("x_lo"), sem("xg_ready")
        pool_sq, pool_acc = sem("pool_sq"), sem("pool_acc")
        stat_mm, stat_ln, rstd_ready = sem("stat_mm"), sem("stat_ln"), sem("rstd_ready")
        out_done, const_ready = sem("out_done"), sem("const_ready")
        dchain, achain = sem("dve_chain"), sem("act_chain")

        PER = dict(ks_ready=2, blk_sum=4, blk_hi=2, blk_lo=2, hid_ready=1, gelu_e=1, hv_ready=1, cmp_mm=1,
                   kc_sq=1, kc_ready=1, kc_mm=1, kc_rstd=1, kc_done=1,
                   nz=1, n_sq=1, n_mean=1, n_rstd=1, n_g=1, n_rot=1, n_rope=1, nv_t=1, nv_ev=1, ng_t=1, ng_e=1, ng_done=1,
                   cs_mm=2, cs_ready=2, cs_max=2, cs_exp=2, cs_p=2, cs_t=2, cs_ev=2,
                   s_mm=32, s_max=32, s_exp=32, s_p=32, p_t=32, p_ev=32, o_half=16, o_mm=16, o_hi=16, o_lo=16,
                   r_rot=1, r_rope=1, r_vt=1, r_vev=1, r_in=4, r_dec=4, r_o=1, r_sq=1, r_mm=1, r_rstd=1, r_gate=1, r_fin=1, r_hi=1, r_lo=1,
                   w_mix=1, w_tanh=1, w_tw=1, w_sgx=1, w_xg=1, w_lr=1, w_e=1, w_sig=1, w_g=1, w_scan=1, w_pow=1, w_kk=1, w_kk2=1, w_kkmm=1,
                   w_kmax=1, w_krs=1, w_rk=1, w_bmm=1, w_bv=1, w_til=1, w_vt=1, w_vev=1, w_bz=1, w_bkt=2, w_bkev=2, w_bd=2,
                   w_l=4, w_lm=4, w_nm=24, w_am=4, w_ae=4, w_pm=20, w_pe=20, w_bm=20, w_be=20, w_xz=2,
                   w_x=4, w_xe=4, w_u=4, w_ue=4, w_s=4, w_se=4, w_y=2, w_ysum=2, w_ysq=2, w_yvar=2, w_yrs=2, w_yn=2, w_yt=2, w_yb=2, w_hi=2, w_lo=2)

        def up(ins, name):
            assert name in PER
            return ins.then_inc(sem(name), 1)

        def need(eng, name, l, k=None):
            eng.wait_ge(sem(name), l * PER[name] + (PER[name] if k is None else k))

        def J_in(l): return l * LAYER_SLABS
        def J_cmp(l): return J_in(l) + N_IN
        def J_out(l): return J_cmp(l) + N_CMP
        def J_up(l, g): return J_out(l) + N_OUT + 32 * g
        def J_down(l, g): return J_up(l, g) + 16

        def walk(eng, J0, count, body):
            body(0, J0, 0)
            loops = (count - 1) // 4
            if loops > 1:
                with eng.Fori(0, loops) as i:
                    for s in range(4):
                        body(1 + s, J0 + 1 + s, i)
            for n in range(1 + 4 * loops if loops > 1 else 1, count):
                body(n, J0 + n, 0)

        block = ctx.enter_context(nc.Block())

        @block.sync
        def _(sp):
            sp.dma_start(VV_t[:, :], vecs).then_inc(vec_in, 16)
            for q in range(4):
                sp.dma_start(X_t[:, q * 1024:(q + 1) * 1024], x_in[:, q * 1024:(q + 1) * 1024]).then_inc(x_in_s, 16)

            def load(s, i):
                dst = raw_t[:, (s % RING) * KT * 128:(s % RING + 1) * KT * 128]
                src = slabs[s, :, :] if isinstance(i, int) else slabs[bass.ds(i * 4 + s, 1), :, :].rearrange("a p n -> (a p) n")
                sp.dma_start(dst, src).then_inc(raw_in[s % RING], 16)

            load(0, 0)
            sp.dma_start(CM_t[:, :], consts).then_inc(con_in, 16)
            for s in range(1, RING):
                load(s, 0)
            loops = (SLABS - RING) // 4
            with sp.Fori(0, loops) as i:
                for s in range(RING):
                    sp.wait_ge(lo_ready, i * 8 + (2 * s + 2))
                    load(RING + s, i)
            for j in range(RING + loops * 4, SLABS):
                sp.wait_ge(lo_ready, 2 * (j - RING) + 2)
                load(j, 0)
            for q in range(4):
                sp.wait_ge(evac_done, J_down(DEPTH - 1, N_GRP - 1) + 4 * q + 4)
                sp.dma_start(out[:, q * 1024:(q + 1) * 1024], X_t[:, q * 1024:(q + 1) * 1024]).then_inc(out_done, 16)
            sp.wait_ge(out_done, 64)

        @block.gpsimd
        def _(pool):
            def square(k, n, i, first):
                x = X_t[:, bass.ds(i * T + n * T, T)] if not isinstance(i, int) else X_t[:, n * T:(n + 1) * T]
                pool.tensor_tensor(psq_t[:, :], x, x, ALU.mult).then_inc(pool_sq, 1)
                pool.wait_ge(pool_sq, i + (k + 1))
                if first:
                    pool.tensor_copy(acc_t[:, :], psq_t[:, :]).then_inc(pool_acc, 1)
                else:
                    pool.tensor_tensor(acc_t[:, :], acc_t[:, :], psq_t[:, :], ALU.add).then_inc(pool_acc, 1)
                pool.wait_ge(pool_acc, i + (k + 1))

            for nm in range(2 * DEPTH):
                if nm == 0:
                    pool.wait_ge(x_in_s, 64)
                else:
                    pool.wait_ge(x_upd, 16 * (nm - 1) + 1)
                    pool.wait_ge(stat_mm, nm)
                square(16 * nm, 0, 0, True)
                with pool.Fori(0, 15) as i:
                    if nm:
                        pool.wait_ge(x_upd, i + (16 * (nm - 1) + 2))
                    square(16 * nm + 1, 1, i, False)

        @block.scalar
        def _(act):
            acount = [0]

            def link(ins):
                acount[0] += 1
                ins.then_inc(achain, 1)
                act.wait_ge(achain, acount[0])

            def split_hi(s, i):
                act.wait_ge(raw_in[s % RING], i * 16 + 16 * (s // RING + 1))
                for a in range(2):
                    h = 2 * s + a
                    if h >= 4:
                        act.wait_ge(half_done, i * 8 + (h - 3))
                    act.activation(hi_t[:, (h % 4) * 1024:(h % 4) * 1024 + 1024],
                                   raw_t[:, (s % RING) * 2048 + a * 1024:(s % RING) * 2048 + a * 1024 + 1024],
                                   ACT.Copy).then_inc(hi_ready, 1)

            def phase(J0, count, evac_hi, w=T, ahead=0):
                def body(n, s, i):
                    if s + 2 < SLABS and n < count - ahead:
                        split_hi(s + 2, i)
                    act.wait_ge(half_done, i * 8 + (2 * s + 2))
                    if s >= 2:
                        act.wait_ge(sum_ready, i * 4 + (s - 1))
                    act.activation(bc_t[:, (s % 2) * T:(s % 2) * T + w], PS_t[:, s % RING, w:2 * w], ACT.Copy).then_inc(bc_ready, 1)
                    if evac_hi:
                        evac_hi(n, i)
                walk(act, J0, count, body)

            def dyn(t, c, k, i, w):
                return t[:, c:c + w] if isinstance(i, int) else t[:, bass.ds(i * k + c, w)]

            def x_hi_step(nm, l, gname, dst):
                def f(n, i):
                    act.wait_ge(xg_ready, i * 4 + (16 * (nm - 1) + n + 1))
                    act.activation(dyn(dst, n * 512, 2048, i, 256), t_t[:, :], ACT.Copy).then_inc(x_hi, 1)
                return f

            def u_hi_step(l, g):
                def f(n, i):
                    act.wait_ge(up_sq, i * 4 + (64 * l + 16 * g + n + 1))
                    act.activation(dyn(U_t, n * 512, 2048, i, 256), sq_t[:, :], ACT.Copy).then_inc(u_hi, 1)
                return f

            def stats(nm):
                act.wait_ge(stat_mm, nm + 1)
                act.activation(rstd_t[:, :], PS_t[:, 4, 0:T], ACT.Ln, bias=eps(E_RMS)).then_inc(stat_ln, 1)
                act.wait_ge(stat_ln, nm + 1)
                act.activation(rstd_t[:, :], rstd_t[:, :], ACT.Exp, scale=-0.5).then_inc(rstd_ready, 1)

            def cmp_prep(l):
                act.wait_ge(half_done, 2 * J_cmp(l))
                for kv in range(2):
                    need(act, "blk_sum", l, 2 * kv + 2)
                    B = BLK_t[:, kv * 1920:(kv + 1) * 1920].rearrange("p (r c) -> p r c", c=120)
                    up(act.activation(B[:, :, 0:60], RA[:, 6144 + 1024 * kv:6144 + 1024 * kv + 960].rearrange("p (r c) -> p r c", c=60),
                                      ACT.Copy), "blk_hi")

            def nsa(l):
                need(act, "hid_ready", l)
                up(act.activation(RB[:, 256:496], RB[:, 256:496], ACT.Exp, scale=-1.5957691216057308), "gelu_e")
                need(act, "cmp_mm", l)
                up(act.activation(RB[:, 512:572], PS_t[:, 4, 0:60], ACT.Square), "kc_sq")
                need(act, "kc_mm", l)
                link(act.activation(RB[:, 512:572], PS_t[:, 4, 64:124], ACT.Ln, bias=eps(E_RMS)))
                up(act.activation(RB[:, 512:572], RB[:, 512:572], ACT.Exp, scale=-0.5), "kc_rstd")
                need(act, "nz", l)
                for b in range(6):
                    ins = act.activation(RB[:, 3072 + 512 * b:3584 + 512 * b], P_t[:, (NS_Q + 2 * b) * T:(NS_Q + 2 * b + 2) * T], ACT.Square)
                up(ins, "n_sq")
                need(act, "n_mean", l)
                for b in range(6):
                    ins = act.activation(RB[:, 512 * b:512 * b + 512], bankc(b, 512), ACT.Ln, bias=eps(E_RMS))
                link(ins)
                act.activation(RB[:, 0:2048], RB[:, 0:2048], ACT.Exp, scale=-0.5, bias=eps(E_LN8))
                up(act.activation(RB[:, 2048:3072], RB[:, 2048:3072], ACT.Exp, scale=-0.5), "n_rstd")
                need(act, "ng_t", l)
                need(act, "n_rope", l)
                G = RB[:, 5120:5216].rearrange("p (a g) -> p a g", g=48)
                up(act.activation(G, PS_t[:, 6, 0:256].rearrange("p (a c) -> p a c", c=128)[:, :, 64:112], ACT.Exp, scale=-1.0), "ng_e")
                need(act, "nv_t", l)
                for tt in range(2):
                    ins = act.activation(RB[:, 1024 + 512 * tt:1536 + 512 * tt], bankc(4 + tt, 512), ACT.Copy)
                up(ins, "nv_ev")
                for tt in range(2):
                    need(act, "cs_max", l, tt + 1)
                    up(act.activation(RB[:, 4096 + 256 * tt:4352 + 256 * tt], RB[:, 4096 + 256 * tt:4352 + 256 * tt], ACT.Exp), "cs_exp")
                for tt in range(2):
                    need(act, "cs_t", l, tt + 1)
                    up(act.activation(RB[:, 4608 + 256 * tt:4864 + 256 * tt], PS_t[:, 2, 0:256], ACT.Copy), "cs_ev")

                def exps(u):
                    tt, w = UN[u][1], 128 * (UN[u][1] + 1)
                    need(act, "s_max", l, u + 1)
                    S = RB[:, 2048 + 512 * (u % 2):2560 + 512 * (u % 2)]
                    mx = RB[:, 5216 + 8 * (u % 4):5224 + 8 * (u % 4)]
                    for h in range(2):
                        ins = act.activation(S[:, h * w:(h + 1) * w], S[:, h * w:(h + 1) * w], ACT.Exp, bias=mx[:, h:h + 1],
                                             accum_out=mx[:, 2 + h:3 + h])
                    up(ins, "s_exp")

                def evac(u):
                    tt = UN[u][1]
                    need(act, "p_t", l, u + 1)
                    if u >= 2:
                        need(act, "o_mm" if u % 2 else "o_half", l, u // 2)
                    n = 256 * (tt + 1)
                    up(act.activation(RB[:, 3072 + 512 * (u % 2):3072 + 512 * (u % 2) + n], PS_t[:, 2 + u % 2, 0:n], ACT.Copy), "p_ev")

                def ohi(v):
                    qt, tt = v // 2, v % 2
                    need(act, "o_mm", l, v + 1)
                    up(act.activation(F0_t[:, (M_NS + qt) * 512 + tt * 128:(M_NS + qt) * 512 + tt * 128 + 128],
                                      PS_t[:, 4 + v % 2, 0:128], ACT.Copy), "o_hi")

                for u in range(32 + 2):
                    if u < 32:
                        exps(u)
                    if u >= 1 and u - 1 < 32:
                        evac(u - 1)
                    if u >= 2 and (u - 2) % 2 == 1:
                        ohi((u - 2) // 2)

            def retention(l):
                need(act, "r_vt", l)
                for tt in range(2):
                    ins = act.activation(RB[:, 3584 + 512 * tt:4096 + 512 * tt], bankc(4 + tt, 512), ACT.Copy)
                up(ins, "r_vev")
                up(act.activation(RB[:, 6656:7680], P_t[:, RT_G * T:(RT_G + 4) * T], ACT.Exp, scale=-1.0), "r_gate")
                need(act, "r_o", l)
                for b in range(2):
                    ins = act.activation(RB[:, 4608 + 512 * b:5120 + 512 * b], bankc(6 + b, 512), ACT.Square)
                up(ins, "r_sq")
                need(act, "r_mm", l)
                for b in range(2):
                    ins = act.activation(RB[:, 5632 + 512 * b:6144 + 512 * b], bankc(b, 512), ACT.Ln, bias=eps(E_RMS))
                link(ins)
                up(act.activation(RB[:, 5632:6656], RB[:, 5632:6656], ACT.Exp, scale=-0.5), "r_rstd")
                need(act, "r_fin", l)
                F = F0_t[:, M_RT * 512:(M_RT + 4) * 512].rearrange("p (k c) -> p k c", c=512)
                up(act.activation(F[:, :, 0:256], RB[:, 4608:5632].rearrange("p (k t) -> p k t", t=256), ACT.Copy), "r_hi")

            def rwkv(l):
                need(act, "w_mix", l)
                if l == 0:
                    act.dma_start(v_first, P_t[:, RW_V * T:(RW_V + 4) * T]).then_inc(sem("vf_out"), 16)
                else:
                    act.dma_start(VF_t, v_first).then_inc(sem("vf_in"), 16)
                up(act.activation(P[:, RW_W, :], P[:, RW_W, :], ACT.Tanh), "w_tw")
                up(act.activation(P_t[:, RW_G * T:(RW_G + 2) * T], P_t[:, RW_G * T:(RW_G + 2) * T], ACT.Sigmoid), "w_xg")
                need(act, "w_lr", l)
                for b, (dst, bias) in enumerate([(0, "w0"), (1024, "a0"), (2048, "v0")][:3 if l else 2]):
                    for c in range(4):
                        ins = act.activation(RB[:, dst + 256 * c:dst + 256 * c + 256], PS_t[:, 2 * b + c // 2, (c % 2) * 256:(c % 2) * 256 + 256],
                                             ACT.Sigmoid, bias=vec(l, bias, c))
                up(ins, "w_e")
                for b in range(2):
                    ins = act.activation(PD[:, 512 * b:512 * b + 512], bankc(6 + b, 512), ACT.Copy)
                up(ins, "w_g")
                need(act, "w_scan", l)
                act.activation(PD[:, 3072:4096], PD[:, 2048:3072], ACT.Exp, scale=-KAPPA)
                act.activation(PD[:, 4096:5120], PD[:, 2048:3072], ACT.Exp, scale=KAPPA)
                up(act.activation(PD[:, 5120:6144], RB[:, 0:1024], ACT.Exp, scale=-KAPPA), "w_pow")
                need(act, "w_kk", l)
                up(act.activation(RB[:, 4096:5120], RB[:, 3072:4096], ACT.Square), "w_kk2")
                need(act, "w_kmax", l)
                link(act.activation(RB[:, 4096:5120], RB[:, 4096:5120], ACT.Ln, scale=65536.0))
                up(act.activation(RB[:, 4096:5120], RB[:, 4096:5120], ACT.Exp, scale=-0.5, bias=eps(E_KK)), "w_krs")
                need(act, "w_vt", l)
                for tt in range(2):
                    ins = act.activation(P_t[:, RW_W * T + 512 * tt:RW_W * T + 512 * tt + 512], bankc(tt, 512), ACT.Copy)
                up(ins, "w_vev")
                act.wait_ge(sem("vf_out"), 16)
                for tt in range(2):
                    need(act, "w_bkt", l, tt + 1)
                    for q in range(2):
                        ins = act.activation(P_t[:, RW_V * T + 512 * q:RW_V * T + 512 * q + 512], bankc(2 + q, 512), ACT.Copy)
                    up(ins, "w_bkev")
                    for s in range(1, 6):
                        for q in range(2):
                            need(act, "w_pm", l, 10 * tt + 2 * (s - 1) + q + 1)
                            up(act.activation(RB[:, 6144 + 512 * q:6656 + 512 * q], bankc(q, 512), ACT.Copy), "w_pe")
                    for c in range(2):
                        r = slice(64 * c, 64 * c + 64)
                        ch = 2 * tt + c
                        need(act, "w_x", l, ch + 1)
                        up(act.activation(RB[r, 0:512], PS_t[r, 0, :], ACT.Copy), "w_xe")
                        need(act, "w_u", l, ch + 1)
                        up(act.activation(RB[r, 512:1024], PS_t[r, 1, :], ACT.Copy), "w_ue")
                    need(act, "w_ysum", l, tt + 1)
                    up(act.activation(RB[:, 6656:7168], RB[:, 6144:6656], ACT.Square), "w_ysq")
                    need(act, "w_yvar", l, tt + 1)
                    link(act.activation(RB[:, 7184:7192], RB[:, 7176:7184], ACT.Ln, scale=1.0 / 64, bias=eps(E_GN)))
                    up(act.activation(RB[:, 7184:7192], RB[:, 7184:7192], ACT.Exp, scale=-0.5), "w_yrs")
                    need(act, "w_yb", l, tt + 1)
                    F = F0_t[:, M_RW * 512:(M_RW + 4) * 512].rearrange("p (k c) -> p k c", c=512)
                    up(act.activation(F[:, :, tt * 128:tt * 128 + 128], RB[:, 6144:6656].rearrange("p (k t) -> p k t", t=128), ACT.Copy), "w_hi")

            act.wait_ge(vec_in, 16)
            act.wait_ge(x_in_s, 64)
            for n in range(KT):
                act.activation(F0_t[:, n * 512:n * 512 + 256], X_t[:, n * T:(n + 1) * T], ACT.Copy, scale=vec(0, "g1", n)).then_inc(x_hi, 1)
            split_hi(0, 0)
            split_hi(1, 0)
            act.wait_ge(const_ready, 1)
            for l in range(DEPTH):
                if l:
                    act.wait_ge(half_done, 2 * J_in(l))
                act.dma_start(LW_t[:, :], small[l, :, :]).then_inc(sem("small_in"), 16)
                act.dma_start(CW_t[:, :], cmpw[l, :, :]).then_inc(sem("cw_in"), 16)
                stats(2 * l)
                phase(J_in(l), N_IN, None)
                cmp_prep(l)
                phase(J_cmp(l), N_CMP, None, w=60, ahead=2)
                nsa(l)
                retention(l)
                rwkv(l)
                need(act, "w_lo", l)
                split_hi(J_out(l), 0)
                split_hi(J_out(l) + 1, 0)
                phase(J_out(l), N_OUT, x_hi_step(2 * l + 1, l, "g2", F1_t))
                stats(2 * l + 1)
                for g in range(N_GRP):
                    phase(J_up(l, g), 16, u_hi_step(l, g))
                    norm = g == N_GRP - 1 and l + 1 < DEPTH
                    phase(J_down(l, g), 16, x_hi_step(2 * l + 2, l + 1, "g1", F0_t) if norm else None)

        @block.vector
        def _(dve):
            dcount = [0]

            def link(ins):
                dcount[0] += 1
                ins.then_inc(dchain, 1)
                dve.wait_ge(dchain, dcount[0])

            def split_lo(s, i, a):
                h = 2 * s + a
                dve.wait_ge(hi_ready, i * 8 + (h + 1))
                c = (h % 4) * 1024
                dve.tensor_tensor(lo_t[:, c:c + 1024], raw_t[:, (s % RING) * 2048 + a * 1024:(s % RING) * 2048 + a * 1024 + 1024],
                                  hi_t[:, c:c + 1024].bitcast(f32), ALU.subtract).then_inc(lo_ready, 1)

            def dyn(t, c, k, i, w):
                return t[:, c:c + w] if isinstance(i, int) else t[:, bass.ds(i * k + c, w)]

            def phase(J0, count, evac, w=T, ahead=0):
                def body(n, s, i):
                    split = s + 2 < SLABS and n < count - ahead
                    if split:
                        split_lo(s + 2, i, 0)
                    dve.wait_ge(bc_ready, i * 4 + (s + 1))
                    if s:
                        dve.wait_ge(evac_done, i * 4 + s)
                    dve.tensor_tensor(s_t[:, 0:w], PS_t[:, s % RING, 0:w], bc_t[:, (s % 2) * T:(s % 2) * T + w], ALU.add).then_inc(sum_ready, 1)
                    if split:
                        split_lo(s + 2, i, 1)
                    dve.wait_ge(sum_ready, i * 4 + (s + 1))
                    evac(n, i)
                walk(dve, J0, count, body)

            def proj_evac(l):
                def f(n, i):
                    dve.tensor_tensor(dyn(P_t, n * T, 4 * T, i, T), s_t[:, :], rstd_t[:, :], ALU.mult).then_inc(evac_done, 1)
                return f

            def cmp_evac(l):
                def f(n, i):
                    dve.tensor_copy(HID[:, 60 * n:60 * n + 60], s_t[:, 0:60]).then_inc(evac_done, 1)
                return f

            def up_evac(l, g):
                def f(n, i):
                    u = 64 * l + 16 * g + n
                    dve.tensor_tensor(t_t[:, :], s_t[:, :], rstd_t[:, :], ALU.mult).then_inc(up_scaled, 1)
                    dve.wait_ge(up_scaled, i * 4 + (u + 1))
                    dve.scalar_tensor_tensor(out=sq_t[:, :], in0=t_t[:, :], scalar=0.0, in1=t_t[:, :], op0=ALU.max, op1=ALU.mult).then_inc(up_sq, 1)
                    dve.wait_ge(u_hi, i * 4 + (u + 1))
                    dve.tensor_tensor(dyn(U_t, n * 512 + 256, 2048, i, 256), sq_t[:, :], dyn(U_t, n * 512, 2048, i, 256).bitcast(f32),
                                      ALU.subtract).then_inc(evac_done, 1)
                return f

            def x_evac(nm, l, gname, dst, norm):
                def f(n, i):
                    k = 16 * (nm - 1) + n if nm else 0
                    ins = dve.tensor_tensor(dyn(X_t, n * T, 4 * T, i, T), s_t[:, :], dyn(X_t, n * T, 4 * T, i, T), ALU.add)
                    ins.then_inc(x_upd if norm else evac_done, 1)
                    if norm:
                        dve.wait_ge(x_upd, i * 4 + (k + 1))
                        g0 = l * NVEC + VEC[gname][0]
                        dve.tensor_scalar(t_t[:, :], dyn(X_t, n * T, 4 * T, i, T), dyn(VV_t, g0 + n, 4, i, 1), None, ALU.mult).then_inc(xg_ready, 1)
                        dve.wait_ge(x_hi, i * 4 + (k + 17))
                        dve.tensor_tensor(dyn(dst, n * 512 + 256, 2048, i, 256), t_t[:, :], dyn(dst, n * 512, 2048, i, 256).bitcast(f32),
                                          ALU.subtract).then_inc(evac_done, 1)
                return f

            def cmp_prep(l):
                dve.wait_ge(half_done, 2 * J_cmp(l))
                dve.wait_ge(evac_done, J_cmp(l))
                for kv, src in enumerate([NS_KC, NS_VC]):
                    K = RA[:, 4096 + 1024 * kv:5120 + 1024 * kv].rearrange("p (g t) -> p g t", t=T)
                    for g in range(4):
                        r = slice(64 * (g % 2), 64 * (g % 2) + 64)
                        dve.tensor_copy(K[0:64, g, :], P[r, src + g // 2, :])
                        ins = dve.tensor_copy(K[64:128, g, 0:255], P[r, src + g // 2, 1:256])
                    up(ins, "ks_ready")
                    need(dve, "ks_ready", l, kv + 1)
                    V = K.rearrange("p g (n r) -> p r g n", r=16)
                    O = RA[:, 6144 + 1024 * kv:6144 + 1024 * kv + 960].rearrange("p (r g n) -> p r g n", g=4, n=15)
                    pe = VV_t[:, l * NVEC + VEC["pe_k" if kv == 0 else "pe_v"][0]:][:, 0:16]
                    for half in range(2):
                        for g in range(4):
                            ins = dve.tensor_tensor(O[:, 8 * half:8 * half + 8, g, :], V[:, 0:16:2, g, half:half + 15],
                                                    pe[:, 8 * half:8 * half + 8].unsqueeze(2).to_broadcast([128, 8, 15]), ALU.add)
                        up(ins, "blk_sum")
                for kv in range(2):
                    need(dve, "blk_hi", l, kv + 1)
                    B = BLK_t[:, kv * 1920:(kv + 1) * 1920].rearrange("p (r c) -> p r c", c=120)
                    up(dve.tensor_tensor(B[:, :, 60:120], RA[:, 6144 + 1024 * kv:6144 + 1024 * kv + 960].rearrange("p (r c) -> p r c", c=60),
                                         B[:, :, 0:60].bitcast(f32), ALU.subtract), "blk_lo")

            def nsa(l):
                dve.wait_ge(evac_done, J_out(l))
                dve.wait_ge(half_done, 2 * J_out(l))
                H = HID[:, 0:240]
                link(dve.tensor_tensor(RB[:, 0:240], H, H, ALU.mult))
                link(dve.tensor_scalar(RB[:, 0:240], RB[:, 0:240], 0.044715, 1.0, ALU.mult, ALU.add))
                up(dve.tensor_tensor(RB[:, 256:496], RB[:, 0:240], H, ALU.mult), "hid_ready")
                need(dve, "gelu_e", l)
                link(dve.tensor_scalar(RB[:, 256:496], RB[:, 256:496], 1.0, None, ALU.add))
                link(dve.reciprocal(RB[:, 256:496], RB[:, 256:496]))
                link(dve.tensor_tensor(HID[:, 256:496], H, RB[:, 256:496], ALU.mult))
                HV = RA[:, 0:512]
                link(dve.memset(HV, 0.0))
                for ht in range(2):
                    for pg in range(2):
                        src = HID[:, 256 + 120 + 60 * ht + 30 * pg:256 + 120 + 60 * ht + 30 * pg + 30].rearrange("p (h n) -> p h n", n=15)
                        for q4 in range(4):
                            o = ht * 256 + pg * 128 + q4 * 32
                            ins = dve.tensor_copy(HV[:, o:o + 32].rearrange("p (h n) -> p h n", n=16)[:, :, 0:15], src)
                up(ins, "hv_ready")
                need(dve, "kc_sq", l)
                link(dve.tensor_scalar(RB[:, 640:700], PS_t[:, 4, 0:60], vec(l, "kn_c"), None, ALU.mult))
                up(dve.memset(KTC_t[:, :], 0.0), "kc_ready")
                need(dve, "kc_mm", l)
                need(dve, "kc_rstd", l)

                def g4(ap):
                    return ap.rearrange("p (g n) -> p g n", n=15)
                cosb = con("cos_c")[:, 0:15].unsqueeze(1).to_broadcast([128, 4, 15])
                sinb = con("sin_c")[:, 0:15].unsqueeze(1).to_broadcast([128, 4, 15])
                dve.tensor_tensor(g4(RB[:, 700:760]), g4(RB[:, 640:700]), cosb, ALU.mult)
                link(dve.tensor_tensor(g4(RB[:, 768:828]), g4(PS_t[:, 4, 128:188]), sinb, ALU.mult))
                link(dve.tensor_tensor(RB[:, 700:760], RB[:, 700:760], RB[:, 768:828], ALU.add))
                KC = KTC_t[:, :].rearrange("p (a h n) -> p a h n", h=2, n=16)
                for h in range(2):
                    r = slice(64 * h, 64 * h + 64)
                    a = RB[r, 700:760].rearrange("p (a h n) -> p a h n", h=2, n=15)[:, :, h, :]
                    b = RB[r, 512:572].rearrange("p (a h n) -> p a h n", h=2, n=15)[:, :, h, :]
                    ins = dve.tensor_tensor(KC[r, :, h, 0:15], a, b, ALU.mult)
                up(ins, "kc_done")
                VZ = RA[:, 512:1536]
                for pg in range(2):
                    ins = dve.tensor_tensor(VZ[:, pg * 512:(pg + 1) * 512].rearrange("p (s d) -> p s d", d=64),
                                            PS_t[:, 4, 256 + 64 * pg:320 + 64 * pg].unsqueeze(1).to_broadcast([128, 8, 64]),
                                            con("vcz").unsqueeze(2).to_broadcast([128, 8, 64]), ALU.mult)
                up(ins, "nz")
                need(dve, "n_sq", l)
                PQ = P_t[:, NS_Q * T:(NS_Q + 12) * T]
                dve.tensor_scalar(PQ[:, 0:2048], PQ[:, 0:2048], vec(l, "qn"), None, ALU.mult)
                dve.tensor_scalar(PQ[:, 2048:2560], PQ[:, 2048:2560], vec(l, "kn_s"), None, ALU.mult)
                up(dve.tensor_scalar(PQ[:, 2560:3072], PQ[:, 2560:3072], vec(l, "kn_w"), None, ALU.mult), "n_g")
                need(dve, "n_rot", l)
                sb_ = con("sin_n").unsqueeze(1).to_broadcast([128, 2, 256])
                for b in range(6):
                    ins = dve.tensor_tensor(RB[:, 3072 + 512 * b:3584 + 512 * b].rearrange("p (a t) -> p a t", t=T),
                                            bankc(b, 512).rearrange("p (a t) -> p a t", t=T), sb_, ALU.mult)
                link(ins)
                PQ3 = PQ.rearrange("p (a t) -> p a t", t=T)
                link(dve.tensor_tensor(PQ3, PQ3, con("cos_n").unsqueeze(1).to_broadcast([128, 12, 256]), ALU.mult))
                link(dve.tensor_tensor(PQ, PQ, RB[:, 3072:6144], ALU.add))
                need(dve, "n_rstd", l)
                dve.tensor_tensor(PQ[:, 0:2048], PQ[:, 0:2048], RB[:, 0:2048], ALU.mult)
                link(dve.memset(RB[:, 6144:8192], 0.0))
                for b in range(2):
                    KZ = RB[:, 6144 + 1024 * b:7168 + 1024 * b].rearrange("p (a h t) -> p a h t", h=2, t=T)
                    for h in range(2):
                        r = slice(64 * h, 64 * h + 64)
                        ins = dve.tensor_tensor(KZ[r, :, h, :], PQ[r, 2048 + 512 * b:2560 + 512 * b].rearrange("p (a t) -> p a t", t=T),
                                                RB[r, 2048 + 512 * b:2560 + 512 * b].rearrange("p (a t) -> p a t", t=T), ALU.mult)
                up(ins, "n_rope")
                need(dve, "ng_e", l)
                link(dve.tensor_scalar(RB[:, 5120:5216], RB[:, 5120:5216], 1.0, None, ALU.add))
                up(dve.reciprocal(RB[:, 5120:5216], RB[:, 5120:5216]), "ng_done")
                need(dve, "ng_done", l)
                GV = RB[:, 5120:5216].rearrange("p (a h b) -> p a h b", h=16, b=3)
                for tt in range(2):
                    if tt:
                        need(dve, "cs_max", l, tt)
                    need(dve, "cs_mm", l, tt + 1)
                    C = RB[:, 4096 + 256 * tt:4352 + 256 * tt]
                    C3 = C.rearrange("p (h n) -> p h n", n=16)
                    m = con("cmp_add")[:, 16 * tt:16 * tt + 16].unsqueeze(1).to_broadcast([128, 16, 16])
                    link(dve.tensor_tensor(C3, PS_t[:, tt, 0:256].rearrange("p (h n) -> p h n", n=16), m, ALU.add))
                    link(dve.tensor_reduce(RB[:, 5248:5264], C3, AX.X, ALU.max))
                    up(dve.tensor_tensor(C3, C3, RB[:, 5248:5264].unsqueeze(2).to_broadcast([128, 16, 16]), ALU.subtract), "cs_max")
                need(dve, "cs_max", l)
                for tt in range(2):
                    if tt:
                        need(dve, "cs_p", l, tt)
                    need(dve, "cs_exp", l, tt + 1)
                    C3 = RB[:, 4096 + 256 * tt:4352 + 256 * tt].rearrange("p (h n) -> p h n", n=16)
                    vis = con("cmp_vis")[:, 16 * tt:16 * tt + 16].unsqueeze(1).to_broadcast([128, 16, 16])
                    link(dve.tensor_reduce(RB[:, 5248:5264], C3[:, :, 0:15], AX.X, ALU.add))
                    link(dve.reciprocal(RB[:, 5264:5280], RB[:, 5248:5264]))
                    link(dve.tensor_tensor(RB[:, 5280:5296], RB[:, 5264:5280], GV[:, tt, :, 0], ALU.mult))
                    link(dve.tensor_tensor(C3, C3, vis, ALU.mult))
                    up(dve.tensor_tensor(C3, C3, RB[:, 5280:5296].unsqueeze(2).to_broadcast([128, 16, 16]), ALU.mult), "cs_p")

                def maxes(u):
                    qt, tt, br = UN[u]
                    w = 128 * (tt + 1)
                    need(dve, "s_mm", l, u + 1)
                    if u >= 2:
                        need(dve, "p_t", l, u - 1)
                    S = RB[:, 2048 + 512 * (u % 2):2560 + 512 * (u % 2)]
                    mx = RB[:, 5216 + 8 * (u % 4):5224 + 8 * (u % 4)]
                    mask = con("causal")[:, 128 * (1 - tt):256]
                    for h in range(2):
                        ins = dve.tensor_tensor_reduce(S[:, h * w:(h + 1) * w], PS_t[:, u % 2, h * w:(h + 1) * w], mask, 1.0, -3.0e38,
                                                       ALU.add, ALU.max, mx[:, 4 + h:5 + h])
                    link(ins)
                    up(dve.tensor_scalar(mx[:, 0:2], mx[:, 4:6], -1.0, None, ALU.mult), "s_max")

                def probs(u):
                    qt, tt, br = UN[u]
                    w = 128 * (tt + 1)
                    need(dve, "s_exp", l, u + 1)
                    S = RB[:, 2048 + 512 * (u % 2):2560 + 512 * (u % 2)]
                    mx = RB[:, 5216 + 8 * (u % 4):5224 + 8 * (u % 4)]
                    link(dve.reciprocal(mx[:, 6:8], mx[:, 2:4]))
                    link(dve.tensor_tensor(mx[:, 6:8], mx[:, 6:8], GV[:, tt, 2 * qt:2 * qt + 2, 1 + br], ALU.mult))
                    for h in range(2):
                        ins = dve.tensor_scalar(S[:, h * w:(h + 1) * w], S[:, h * w:(h + 1) * w], mx[:, 6 + h:7 + h], None, ALU.mult)
                    up(ins, "s_p")

                def olo(v):
                    qt, tt = v // 2, v % 2
                    need(dve, "o_hi", l, v + 1)
                    c = (M_NS + qt) * 512 + tt * 128
                    up(dve.tensor_tensor(F0_t[:, c + 256:c + 384], PS_t[:, 4 + v % 2, 0:128], F0_t[:, c:c + 128].bitcast(f32), ALU.subtract), "o_lo")

                maxes(0)
                for u in range(32 + 3):
                    if u + 1 < 32:
                        maxes(u + 1)
                    if u < 32:
                        probs(u)
                    if u >= 3 and (u - 3) % 2 == 1:
                        olo((u - 3) // 2)

            def retention(l):
                PR = P_t[:, RT_Q * T:(RT_Q + 8) * T]
                PR3 = PR.rearrange("p (a t) -> p a t", t=T)
                need(dve, "r_rot", l)
                sb_ = con("sin_r").unsqueeze(1).to_broadcast([128, 2, 256])
                for b in range(4):
                    ins = dve.tensor_tensor(RB[:, 512 * b:512 * b + 512].rearrange("p (a t) -> p a t", t=T),
                                            bankc(b, 512).rearrange("p (a t) -> p a t", t=T), sb_, ALU.mult)
                link(dve.tensor_tensor(PR3, PR3, con("cos_r").unsqueeze(1).to_broadcast([128, 8, 256]), ALU.mult))
                up(dve.tensor_tensor(PR, PR, RB[:, 0:2048], ALU.add), "r_rope")
                need(dve, "r_gate", l)
                link(dve.tensor_scalar(RB[:, 6656:7680], RB[:, 6656:7680], 1.0, None, ALU.add))
                link(dve.reciprocal(RB[:, 6656:7680], RB[:, 6656:7680]))
                link(dve.tensor_tensor(RB[:, 6656:7680], RB[:, 6656:7680], P_t[:, RT_G * T:(RT_G + 4) * T], ALU.mult))
                for h in range(4):
                    need(dve, "r_in", l, h + 1)
                    dec = con("decay")[:, 256 * h:256 * h + 256]
                    I = RB[:, 2048 + 384 * h:2432 + 384 * h]
                    dve.tensor_tensor(I[:, 0:256], PS_t[:, h, 0:256], dec, ALU.mult)
                    up(dve.tensor_tensor(I[:, 256:384], PS_t[:, h, 256:384], dec[:, 0:128], ALU.mult), "r_dec")
                need(dve, "r_rstd", l)
                link(dve.tensor_tensor(RB[:, 6656:7680], RB[:, 6656:7680], RB[:, 5632:6656], ALU.mult))
                for b in range(2):
                    ins = dve.tensor_tensor(RB[:, 4608 + 512 * b:5120 + 512 * b], bankc(6 + b, 512), RB[:, 6656 + 512 * b:7168 + 512 * b], ALU.mult)
                up(ins, "r_fin")
                need(dve, "r_hi", l)
                F = F0_t[:, M_RT * 512:(M_RT + 4) * 512].rearrange("p (k c) -> p k c", c=512)
                up(dve.tensor_tensor(F[:, :, 256:512], RB[:, 4608:5632].rearrange("p (k t) -> p k t", t=256), F[:, :, 0:256].bitcast(f32),
                                     ALU.subtract), "r_lo")

            def rwkv(l):
                D3 = RB[:, 0:17 * T].rearrange("p (a t) -> p a t", t=T)
                P3 = P[:, 0:17, :]
                dve.tensor_tensor(D3[:, :, 1:T], P3[:, :, 0:T - 1], P3[:, :, 1:T], ALU.subtract)
                link(dve.tensor_scalar(D3[:, :, 0:1], P3[:, :, 0:1], -1.0, None, ALU.mult))
                for a in range(17):
                    ins = dve.scalar_tensor_tensor(out=P[:, a, :], in0=D3[:, a, :], scalar=vec(l, "mix", a), in1=P[:, a, :], op0=ALU.mult, op1=ALU.add)
                up(ins, "w_mix")
                need(dve, "w_mix", l)
                for c in range(4):
                    ins = dve.tensor_scalar(RB[:, 3072 + 256 * c:3328 + 256 * c], P[:, RW_K + c, :], vec(l, "kk", c), None, ALU.mult)
                up(ins, "w_kk")
                need(dve, "w_e", l)
                for c in range(4):
                    ins = dve.tensor_tensor_scan(PD[:, 2048 + 256 * c:2304 + 256 * c], con("scan"), RB[:, 256 * c:256 * c + 256], 0.0, ALU.mult, ALU.add)
                link(ins)
                up(dve.tensor_tensor(RB[:, 0:1024], PD[:, 2048:3072], RB[:, 0:1024], ALU.subtract), "w_scan")
                V, K, R_ = P_t[:, RW_V * T:(RW_V + 4) * T], P_t[:, RW_K * T:(RW_K + 4) * T], P_t[:, RW_R * T:(RW_R + 4) * T]
                if l:
                    dve.wait_ge(sem("vf_in"), 16)
                    link(dve.tensor_tensor(PD[:, 6144:7168], VF_t, V, ALU.subtract))
                    link(dve.tensor_tensor(PD[:, 6144:7168], PD[:, 6144:7168], RB[:, 2048:3072], ALU.mult))
                    link(dve.tensor_tensor(V, V, PD[:, 6144:7168], ALU.add))
                for c in range(4):
                    ins = dve.tensor_scalar(PD[:, 6144 + 256 * c:6400 + 256 * c], RB[:, 1024 + 256 * c:1280 + 256 * c], 1.0, vec(l, "ka", c), ALU.subtract, ALU.mult)
                link(ins)
                link(dve.scalar_tensor_tensor(out=K, in0=PD[:, 6144:7168], scalar=1.0, in1=K, op0=ALU.add, op1=ALU.mult))
                for c in range(4):
                    ins = dve.scalar_tensor_tensor(out=PD[:, 6144 + 256 * c:6400 + 256 * c], in0=P[:, RW_R + c, :], scalar=vec(l, "rk", c), in1=P[:, RW_K + c, :],
                                                   op0=ALU.mult, op1=ALU.mult)
                up(ins, "w_rk")
                need(dve, "w_kkmm", l)
                for b in range(2):
                    ins = dve.tensor_scalar(RB[:, 4096 + 512 * b:4608 + 512 * b], bankc(b, 512), 1e-24, None, ALU.max)
                up(ins, "w_kmax")
                need(dve, "w_pow", l)
                need(dve, "w_kmax", l)
                dve.tensor_copy(WC_t[:, :].rearrange("p (c k) -> p c k", k=4),
                                PD[:, 3072:4096].rearrange("p (c k t) -> p c k t", k=4, t=64)[:, :, :, 63])
                link(dve.tensor_tensor(R_, R_, PD[:, 3072:4096], ALU.mult))
                link(dve.tensor_tensor(K, K, PD[:, 4096:5120], ALU.mult))
                need(dve, "w_krs", l)
                link(dve.tensor_tensor(RB[:, 3072:4096], RB[:, 3072:4096], RB[:, 4096:5120], ALU.mult))
                link(dve.tensor_tensor(RB[:, 1024:2048], RB[:, 1024:2048], RB[:, 3072:4096], ALU.mult))
                dve.tensor_tensor(RB[:, 1024:2048], RB[:, 1024:2048], PD[:, 4096:5120], ALU.mult)
                link(dve.scalar_tensor_tensor(out=RB[:, 3072:4096], in0=RB[:, 3072:4096], scalar=-1.0, in1=PD[:, 5120:6144], op0=ALU.mult, op1=ALU.mult))
                need(dve, "w_bmm", l)
                for b in range(2):
                    ins = dve.tensor_tensor(PD[:, 1024 + 512 * b:1536 + 512 * b], bankc(2 + b, 512), V[:, 512 * b:512 * b + 512], ALU.mult)
                up(ins, "w_bv")
                up(dve.memset(ST_t[:, :], 0.0), "w_til")
                need(dve, "w_til", l)
                up(dve.memset(BD, 0.0), "w_bz")
                need(dve, "w_bz", l)
                BD5 = BD.rearrange("p (c h a t) -> p c h a t", c=4, h=2, a=2)
                for tt in range(2):
                    if tt:
                        need(dve, "w_y", l, tt)
                    for h in range(2):
                        r = slice(64 * h, 64 * h + 64)
                        for a, src in enumerate([RB[r, 3072:4096], P_t[r, RW_R * T:(RW_R + 4) * T]]):
                            s3 = src.rearrange("p (c t) -> p c t", t=T)[:, :, tt * 128:tt * 128 + 128]
                            ins = dve.tensor_copy(BD5[r, :, h, a, :], s3)
                    up(ins, "w_bd")
                    m = con("rw_mask").unsqueeze(1).to_broadcast([128, 2, 256])
                    for q in range(4):
                        need(dve, "w_l", l, 2 * tt + q // 2 + 1)
                        for x, L in enumerate([LB, LK]):
                            b = 2 * (q % 2) + x
                            ins = dve.tensor_tensor(L[:, 512 * q:512 * q + 512].rearrange("p (h w) -> p h w", w=256),
                                                    bankc((4 if q // 2 else 0) + b, 512).rearrange("p (h w) -> p h w", w=256), m, ALU.mult)
                        if q % 2:
                            up(ins, "w_lm")
                    need(dve, "w_lm", l, 2 * tt + 2)
                    LB4 = LB.rearrange("p (h a t) -> p h a t", a=2, t=128)

                    def level_mask(s, q):
                        mk = con("lev")[:, 128 * s:128 * s + 128].unsqueeze(1).to_broadcast([128, 4, 128])
                        up(dve.tensor_tensor(NM[:, 512 * q:512 * q + 512].rearrange("p (h t) -> p h t", t=128), LB4[:, 4 * q:4 * q + 4, 0, :], mk, ALU.mult), "w_nm")
                    idb = con("ident").unsqueeze(1).to_broadcast([128, 4, 128])
                    for q in range(2):
                        level_mask(0, q)
                    for q in range(2):
                        need(dve, "w_am", l, 2 * tt + q + 1)
                        dve.tensor_tensor(TA[:, 512 * q:512 * q + 512].rearrange("p (h t) -> p h t", t=128), bankc(q, 512).rearrange("p (h t) -> p h t", t=128), idb, ALU.add)
                        up(dve.tensor_tensor(TB[:, 512 * q:512 * q + 512].rearrange("p (h t) -> p h t", t=128), NM[:, 512 * q:512 * q + 512].rearrange("p (h t) -> p h t", t=128), idb, ALU.add), "w_ae")
                    for s in range(1, 6):
                        for q in range(2):
                            need(dve, "w_ae", l, 2 * tt + q + 1)
                            if s > 1:
                                need(dve, "w_pm", l, 10 * tt + 2 * (s - 2) + q + 1)
                                need(dve, "w_be", l, 10 * tt + 2 * (s - 2) + q + 1)
                            level_mask(s, q)
                        for q in range(2):
                            k = 10 * tt + 2 * (s - 1) + q + 1
                            need(dve, "w_bm", l, k)
                            if s < 5:
                                dve.tensor_tensor(TA[:, 512 * q:512 * q + 512], TA[:, 512 * q:512 * q + 512], bankc(2 + q, 512), ALU.add)
                            up(dve.tensor_tensor(TB[:, 512 * q:512 * q + 512], TB[:, 512 * q:512 * q + 512], bankc(4 + q, 512), ALU.add), "w_be")
                    need(dve, "w_be", l, 10 * tt + 10)
                    up(dve.memset(TA, 0.0), "w_xz")
                    for c in range(2):
                        ch = 2 * tt + c
                        need(dve, "w_s", l, ch + 1)
                        link(dve.tensor_tensor(SN_t[:, :], PS_t[:, 2, 0:256], ST_t[:, :], ALU.add))
                        up(dve.tensor_tensor(ST_t[:, :].rearrange("p (c i) -> p c i", i=64), SN_t[:, :].rearrange("p (c i) -> p c i", i=64),
                                             WC_t[:, :].rearrange("p (c k) -> p c k", k=4)[:, :, ch:ch + 1].to_broadcast([128, 4, 64]), ALU.mult), "w_se")
                    need(dve, "w_y", l, tt + 1)
                    Y3 = PS_t[:, 3, :].rearrange("p (h i) -> p h i", i=64)
                    YC = RB[:, 6144:6656]
                    YC3 = YC.rearrange("p (h i) -> p h i", i=64)
                    link(dve.tensor_reduce(RB[:, 7168:7176], Y3, AX.X, ALU.add))
                    link(dve.tensor_scalar(RB[:, 7168:7176], RB[:, 7168:7176], 1.0 / 64, None, ALU.mult))
                    up(dve.tensor_tensor(YC3, Y3, RB[:, 7168:7176].unsqueeze(2).to_broadcast([128, 8, 64]), ALU.subtract), "w_ysum")
                    need(dve, "w_ysq", l, tt + 1)
                    up(dve.tensor_reduce(RB[:, 7176:7184], RB[:, 6656:7168].rearrange("p (h i) -> p h i", i=64), AX.X, ALU.add), "w_yvar")
                    need(dve, "w_yrs", l, tt + 1)
                    up(dve.tensor_tensor(RB[:, 6656:7168].rearrange("p (h i) -> p h i", i=64), YC3, RB[:, 7184:7192].unsqueeze(2).to_broadcast([128, 8, 64]), ALU.mult), "w_yn")
                    need(dve, "w_yt", l, tt + 1)
                    for c in range(4):
                        ins = dve.tensor_scalar(RB[:, 6144 + 128 * c:6272 + 128 * c], PS_t[:, 4, 128 * c:128 * c + 128], vec(l, "lng", c), vec(l, "lnb", c), ALU.mult, ALU.add)
                    link(ins)
                    YO = RB[:, 6144:6656].rearrange("p (c t) -> p c t", t=128)
                    tsl = slice(tt * 128, tt * 128 + 128)
                    link(dve.tensor_tensor(YO, YO, PD[:, 1024:2048].rearrange("p (c t) -> p c t", t=T)[:, :, tsl], ALU.add))
                    up(dve.tensor_tensor(YO, YO, PD[:, 0:1024].rearrange("p (c t) -> p c t", t=T)[:, :, tsl], ALU.mult), "w_yb")
                    need(dve, "w_hi", l, tt + 1)
                    F = F0_t[:, M_RW * 512:(M_RW + 4) * 512].rearrange("p (k c) -> p k c", c=512)
                    up(dve.tensor_tensor(F[:, :, 256 + tt * 128:384 + tt * 128], YO, F[:, :, tt * 128:tt * 128 + 128].bitcast(f32), ALU.subtract), "w_lo")
                need(dve, "w_lo", l)

            dve.memset(EPS_t[:, E_RMS:E_RMS + 1], 1e-6)
            dve.memset(EPS_t[:, E_KK:E_KK + 1], 5.545177444479562)
            dve.memset(EPS_t[:, E_LN8:E_LN8 + 1], -2.0794415416798357)
            dve.memset(EPS_t[:, E_GN:E_GN + 1], 64e-5)
            dve.memset(EPS_t[:, 4:8], 0.0).then_inc(const_ready, 1)
            dve.wait_ge(vec_in, 16)
            dve.wait_ge(con_in, 16)
            for n in range(KT):
                dve.wait_ge(x_hi, n + 1)
                dve.scalar_tensor_tensor(out=F0_t[:, n * 512 + 256:n * 512 + 512], in0=X_t[:, n * T:(n + 1) * T], scalar=vec(0, "g1", n),
                                         in1=F0_t[:, n * 512:n * 512 + 256].bitcast(f32), op0=ALU.mult, op1=ALU.subtract).then_inc(x_lo, 1)
                if n % 4 == 3:
                    split_lo(n // 8, 0, n // 4 % 2)
            for l in range(DEPTH):
                dve.wait_ge(rstd_ready, 2 * l + 1)
                phase(J_in(l), N_IN, proj_evac(l))
                cmp_prep(l)
                phase(J_cmp(l), N_CMP, cmp_evac(l), w=60, ahead=2)
                nsa(l)
                retention(l)
                rwkv(l)
                for s in range(2):
                    for a in range(2):
                        split_lo(J_out(l) + s, 0, a)
                phase(J_out(l), N_OUT, x_evac(2 * l + 1, l, "g2", F1_t, True))
                dve.wait_ge(rstd_ready, 2 * l + 2)
                for g in range(N_GRP):
                    phase(J_up(l, g), 16, up_evac(l, g))
                    last = g == N_GRP - 1
                    phase(J_down(l, g), 16, x_evac(2 * l + 2 if last else 0, l + 1, "g1", F0_t, last and l + 1 < DEPTH))

        @block.tensor
        def _(pe):
            def phase(J0, count, rhs, ready, base, w=T, after_first=None):
                def body(n, s, i):
                    slab(n, s, i, rhs, ready, base, w)
                    if n == 0 and after_first:
                        after_first()
                walk(pe, J0, count, body)

            def slab(n, s, i, rhs, ready, base, w):
                    B = PS_t[:, s % RING, :]
                    for a in range(2):
                        h = 2 * s + a
                        pe.wait_ge(lo_ready, i * 8 + (h + 1))
                        if a == 0 and s >= 4:
                            pe.wait_ge(sum_ready, i * 4 + (s - 3))
                        for k8 in range(HALF):
                            k = HALF * a + k8
                            if ready and n == 0 and k in (0, 8, 14, 15):
                                pe.wait_ge(ready, base + {0: 8, 8: 14, 14: 15, 15: 16}[k])
                            c = (h % 4) * 1024 + k8 * 128
                            x = rhs(k)
                            if k == 0:
                                pe.matmul(B[:, 0:2 * w], hi_t[:, c:c + 128], x, start=True, stop=False)
                                pe.matmul(B[:, 0:w], lo_t[:, c:c + 128], x[:, 0:w], start=False, stop=False)
                            else:
                                pe.matmul(B[:, 0:w], lo_t[:, c:c + 128], x[:, 0:w], start=False, stop=False)
                                ins = pe.matmul(B[:, 0:2 * w], hi_t[:, c:c + 128], x, start=False, stop=(k == KT - 1))
                        ins.then_inc(half_done, 1)

            def stats(nm):
                def f():
                    pe.wait_ge(pool_acc, 16 * (nm + 1))
                    pe.matmul(PS_t[:, 4, 0:T], con("one_d"), acc_t[:, :], start=True, stop=True).then_inc(stat_mm, 1)
                return f

            def mm(o, a, b, start=True, stop=True):
                return pe.matmul(o, a, b, start=start, stop=stop, skip_group_check=True)

            def nsa(l):
                need(pe, "hv_ready", l)
                pe.wait_ge(sem("cw_in"), 16 * (l + 1))
                for ht in range(2):
                    mm(PS_t[:, 4, 0:60], CW_t[:, 128 * ht:128 * ht + 128], HID[:, 256 + 60 * ht:316 + 60 * ht], start=ht == 0)
                for pg in range(2):
                    for ht in range(2):
                        ins = mm(PS_t[:, 4, 256 + 64 * pg:320 + 64 * pg], RA[:, ht * 256 + pg * 128:ht * 256 + pg * 128 + 128],
                                 CW_t[:, 256 + 64 * ht:320 + 64 * ht], start=False)
                up(ins, "cmp_mm")
                need(pe, "kc_ready", l)
                mm(PS_t[:, 4, 64:124], con("blk_mean"), RB[:, 512:572], start=False)
                up(mm(PS_t[:, 4, 128:188], con("rot_n"), RB[:, 640:700], start=False), "kc_mm")
                need(pe, "n_sq", l)
                for b in range(6):
                    if b == 4:
                        need(pe, "nz", l)
                    ins = mm(bankc(b, 512), con("blk_mean"), RB[:, 3072 + 512 * b:3584 + 512 * b])
                up(ins, "n_mean")
                for tt in range(2):
                    ins = pe.transpose(PS_t[:, 6, 128 * tt:128 * tt + 128], P[:, RW_X, 128 * tt:128 * tt + 128], con("ident"))
                up(ins, "ng_t")
                need(pe, "n_g", l)
                need(pe, "n_rstd", l)
                for b in range(6):
                    ins = mm(bankc(b, 512), con("rot_n"), P_t[:, (NS_Q + 2 * b) * T:(NS_Q + 2 * b + 2) * T])
                up(ins, "n_rot")
                need(pe, "n_rope", l)
                for tt in range(2):
                    for j in range(4):
                        ins = pe.transpose(PS_t[:, 4 + tt, 128 * j:128 * j + 128], P[:, NS_VS + j, 128 * tt:128 * tt + 128], con("ident"))
                up(ins, "nv_t")
                for tt in range(2):
                    for qt in range(8):
                        ins = mm(PS_t[:, tt, 32 * qt:32 * qt + 32], P[:, NS_Q + qt, 128 * tt:128 * tt + 128], KTC_t[:, 32 * (qt // 4):32 * (qt // 4) + 32], start=qt == 0)
                    up(ins, "cs_mm")
                for tt in range(2):
                    need(pe, "cs_p", l, tt + 1)
                    if tt:
                        need(pe, "cs_ev", l, tt)
                    for j in range(2):
                        ins = pe.transpose(PS_t[:, 2, 128 * j:128 * j + 128], RB[:, 4096 + 256 * tt + 128 * j:4224 + 256 * tt + 128 * j], con("ident"))
                    up(ins, "cs_t")
                need(pe, "cs_ev", l)
                need(pe, "nv_ev", l)

                def scores(u):
                    qt, tt, br = UN[u]
                    w = 128 * (tt + 1)
                    if u >= 2:
                        need(pe, "s_max", l, u - 1)
                    K = RB[:, 6144 + 1024 * br + 512 * (qt // 4):6144 + 1024 * br + 512 * (qt // 4) + 512].rearrange("p (h t) -> p h t", t=T)
                    up(mm(PS_t[:, u % 2, 0:2 * w].rearrange("p (h t) -> p h t", t=w), P[:, NS_Q + qt, 128 * tt:128 * tt + 128], K[:, :, 0:w]), "s_mm")

                def transposes(u):
                    qt, tt, br = UN[u]
                    w = 128 * (tt + 1)
                    need(pe, "s_p", l, u + 1)
                    if u >= 2:
                        need(pe, "p_ev", l, u - 1)
                    S = RB[:, 2048 + 512 * (u % 2):2560 + 512 * (u % 2)]
                    for j in range(2 * (tt + 1)):
                        ins = pe.transpose(PS_t[:, 2 + u % 2, 128 * j:128 * j + 128], S[:, 128 * j:128 * j + 128], con("ident"))
                    up(ins, "p_t")

                def values(u):
                    qt, tt, br = UN[u]
                    v = u // 2
                    need(pe, "p_ev", l, u + 1)
                    O = PS_t[:, 4 + v % 2, 0:128]
                    if u % 2 == 0:
                        if v >= 2:
                            need(pe, "o_lo", l, v - 1)
                        mm(O, RA[:, 512 + 512 * (qt // 4) + 128 * (qt % 4):640 + 512 * (qt // 4) + 128 * (qt % 4)],
                           RB[:, 4608 + 256 * tt + 128 * (qt // 4):4736 + 256 * tt + 128 * (qt // 4)], start=True, stop=False)
                    for h in range(2):
                        g = 2 * (qt // 4) + h
                        for kt in range(tt + 1):
                            V = RB[:, 1024 + 512 * kt + 256 * br + 64 * g:1088 + 512 * kt + 256 * br + 64 * g]
                            ins = mm(O[64 * h:64 * h + 64, :], V, RB[:, 3072 + 512 * (u % 2) + 128 * (h * (tt + 1) + kt):3200 + 512 * (u % 2) + 128 * (h * (tt + 1) + kt)],
                                     start=False, stop=u % 2 == 1)
                    if u % 2:
                        up(ins, "o_mm")
                    else:
                        up(ins, "o_half")

                scores(0)
                for u in range(32 + 1):
                    if u + 1 < 32:
                        scores(u + 1)
                    if u < 32:
                        transposes(u)
                    if u >= 1:
                        values(u - 1)

            def retention(l):
                for b in range(4):
                    ins = mm(bankc(b, 512), con("rot_r"), P_t[:, (RT_Q + 2 * b) * T:(RT_Q + 2 * b + 2) * T])
                up(ins, "r_rot")
                need(pe, "o_lo", l)
                for tt in range(2):
                    for j in range(4):
                        ins = pe.transpose(PS_t[:, 4 + tt, 128 * j:128 * j + 128], P[:, RT_V + j, 128 * tt:128 * tt + 128], con("ident"))
                up(ins, "r_vt")
                need(pe, "r_rope", l)
                for h in range(4):
                    mm(PS_t[:, h, 0:256], P[:, RT_K + h, 0:128], P[:, RT_Q + h, :])
                    up(mm(PS_t[:, h, 256:384], P[:, RT_K + h, 128:256], P[:, RT_Q + h, 128:256], start=False), "r_in")
                need(pe, "r_vev", l)
                for h in range(4):
                    need(pe, "r_dec", l, h + 1)
                    O = PS_t[:, 6 + h // 2, 256 * (h % 2):256 * (h % 2) + 256]
                    I = RB[:, 2048 + 384 * h:2432 + 384 * h]
                    mm(O, RB[:, 3584 + 128 * h:3712 + 128 * h], I[:, 0:256], start=h % 2 == 0, stop=False)
                    ins = mm(O[:, 128:256], RB[:, 4096 + 128 * h:4224 + 128 * h], I[:, 256:384], start=False)
                up(ins, "r_o")
                need(pe, "r_sq", l)
                for b in range(2):
                    ins = mm(bankc(b, 512), con("one_h"), RB[:, 4608 + 512 * b:5120 + 512 * b])
                up(ins, "r_mm")

            def rwkv(l):
                pe.wait_ge(sem("small_in"), 16 * (l + 1))
                need(pe, "r_fin", l)
                need(pe, "w_tw", l)
                w2, a2, v2 = (LW_t[:, LW[n][0]:LW[n][1]] for n in ("w2", "a2", "v2"))
                for b, (w, src) in enumerate([(w2, RW_W), (a2, RW_A), (v2, RW_X)][:3 if l else 2]):
                    for c in range(4):
                        mm(PS_t[:, 2 * b + c // 2, (c % 2) * 256:(c % 2) * 256 + 256], w[:, 128 * c:128 * c + 128], P[:, src, :], start=c % 2 == 0)
                need(pe, "w_xg", l)
                for c in range(4):
                    for k in range(2):
                        g2 = LW_t[:, LW["g2"][0] + 512 * k + 128 * c:LW["g2"][0] + 512 * k + 128 * c + 128]
                        ins = mm(PS_t[:, 6 + c // 2, (c % 2) * 256:(c % 2) * 256 + 256], g2, P[:, RW_G + k, :], start=c % 2 == 0 and k == 0, stop=k == 1)
                up(ins, "w_lr")
                need(pe, "w_kk2", l)
                need(pe, "w_e", l)
                for b in range(2):
                    ins = mm(bankc(b, 512), con("blk_sum"), RB[:, 4096 + 512 * b:4608 + 512 * b])
                up(ins, "w_kkmm")
                need(pe, "w_rk", l)
                for b in range(2):
                    ins = mm(bankc(2 + b, 512), con("blk_sum"), PD[:, 6144 + 512 * b:6656 + 512 * b])
                up(ins, "w_bmm")
                need(pe, "w_til", l)
                for tt in range(2):
                    for c in range(4):
                        ins = pe.transpose(PS_t[:, tt, 128 * c:128 * c + 128], P[:, RW_V + c, 128 * tt:128 * tt + 128], con("ident"))
                up(ins, "w_vt")
                VT = P_t[:, RW_W * T:RW_W * T + 1024]
                BT = P_t[:, RW_V * T:RW_V * T + 512]
                KTt = P_t[:, RW_V * T + 512:RW_V * T + 1024]
                for tt in range(2):
                    ts_ = slice(128 * tt, 128 * tt + 128)
                    need(pe, "w_vev", l)
                    if tt:
                        need(pe, "w_se", l, 2 * tt)
                        need(pe, "w_ysum", l, tt)
                    for c in range(4):
                        pe.transpose(PS_t[:, 2, 128 * c:128 * c + 128], RB[:, 1024 + 256 * c + 128 * tt:1152 + 256 * c + 128 * tt], con("ident"))
                        ins = pe.transpose(PS_t[:, 3, 128 * c:128 * c + 128], P[:, RW_K + c, ts_], con("ident"))
                    up(ins, "w_bkt")
                    need(pe, "w_bd", l, tt + 1)
                    need(pe, "w_bkev", l, tt + 1)
                    if tt:
                        need(pe, "w_yb", l, tt)
                    for c in range(4):
                        rhs = BD[:, 512 * c:512 * c + 512]
                        b0 = (4 if c // 2 else 0) + 2 * (c % 2)
                        mm(bankc(b0, 512), RB[:, 1024 + 256 * c + 128 * tt:1152 + 256 * c + 128 * tt], rhs)
                        ins = mm(bankc(b0 + 1, 512), P[:, RW_K + c, ts_], rhs)
                        if c % 2:
                            up(ins, "w_l")
                    need(pe, "w_lm", l, 2 * tt + 2)
                    for q in range(2):
                        need(pe, "w_nm", l, 12 * tt + q + 1)
                        for h in range(4):
                            o = 512 * q + 128 * h
                            ins = mm(PS_t[:, q, 128 * h:128 * h + 128], NM[:, o:o + 128], con("ident"), start=h == 0)
                        up(ins, "w_am")
                    for s in range(1, 6):
                        for q in range(2):
                            need(pe, "w_nm", l, 12 * tt + 2 * s + q + 1)
                            if s == 1:
                                need(pe, "w_ae", l, 2 * tt + q + 1)
                            else:
                                need(pe, "w_be", l, 10 * tt + 2 * (s - 2) + q + 1)
                            for h in range(4):
                                o = 512 * q + 128 * h
                                ins = mm(PS_t[:, q, 128 * h:128 * h + 128], NM[:, o:o + 128], TA[:, o:o + 128], start=h == 0)
                            up(ins, "w_pm")
                        for q in range(2):
                            k = 10 * tt + 2 * (s - 1) + q + 1
                            need(pe, "w_pe", l, k)
                            for h in range(4):
                                o = 512 * q + 128 * h
                                if s < 5:
                                    mm(PS_t[:, 2 + q, 128 * h:128 * h + 128], TB[:, o:o + 128], PP[:, o:o + 128], start=h == 0)
                                ins = mm(PS_t[:, 4 + q, 128 * h:128 * h + 128], PP[:, o:o + 128], TB[:, o:o + 128], start=h == 0)
                            up(ins, "w_bm")
                    need(pe, "w_xz", l, tt + 1)
                    BD5 = BD.rearrange("p (c h a t) -> p c h a t", c=4, h=2, a=2)
                    LB4 = LB.rearrange("p (h a t) -> p h a t", a=2, t=128)
                    LK4 = LK.rearrange("p (h a t) -> p h a t", a=2, t=128)
                    Y = PS_t[:, 3, :]
                    for h in range(8):
                        mm(Y[:, 64 * h:64 * h + 64], LK4[:, h, 1, :], VT[:, 512 * tt + 64 * h:512 * tt + 64 * h + 64], start=h == 0, stop=False)
                    for c in range(2):
                        ch = 2 * tt + c
                        r = slice(64 * c, 64 * c + 64)
                        if ch:
                            need(pe, "w_se", l, ch)
                        for h in range(8):
                            o = slice(64 * h, 64 * h + 64)
                            S = ST_t[:, 64 * (h // 2):64 * (h // 2) + 64]
                            mm(PS_t[r, 0, o], BD5[:, h // 2, h % 2, 0, r], S, start=h == 0, stop=False)
                            ins = mm(PS_t[r, 0, o], LK4[:, h, 0, r], VT[:, 512 * tt + 64 * h:512 * tt + 64 * h + 64], start=False)
                        up(ins, "w_x")
                        for h in range(8):
                            mm(Y[r, 64 * h:64 * h + 64], BD5[:, h // 2, h % 2, 1, r], ST_t[:, 64 * (h // 2):64 * (h // 2) + 64], start=False, stop=False)
                        need(pe, "w_xe", l, ch + 1)
                        for h in range(8):
                            ins = mm(PS_t[r, 1, 64 * h:64 * h + 64], TB[:, 128 * h + 64 * c:128 * h + 64 * c + 64], TA[:, 64 * h:64 * h + 64], start=h == 0)
                        up(ins, "w_u")
                        need(pe, "w_ue", l, ch + 1)
                        for h in range(8):
                            o = PS_t[64 * (h % 2):64 * (h % 2) + 64, 2, 64 * (h // 2):64 * (h // 2) + 64]
                            hs = slice(64 * h, 64 * h + 64)
                            mm(o, BT[r, hs], TA[r, 512 + 64 * h:576 + 64 * h], start=h < 2, stop=False)
                            ins = mm(o, KTt[r, hs], VT[r, 512 * tt + 64 * h:512 * tt + 64 * h + 64], start=False)
                        up(ins, "w_s")
                    for h in range(8):
                        ins = mm(Y[:, 64 * h:64 * h + 64], LB4[:, h, 1, :], TA[:, 512 + 64 * h:576 + 64 * h], start=False)
                    up(ins, "w_y")
                    need(pe, "w_yn", l, tt + 1)
                    for c in range(4):
                        ins = pe.transpose(PS_t[:, 4, 128 * c:128 * c + 128], RB[:, 6656 + 128 * c:6784 + 128 * c], con("ident"))
                    up(ins, "w_yt")

            pe.wait_ge(con_in, 16)
            for l in range(DEPTH):
                phase(J_in(l), N_IN, lambda k: F0_t[:, 512 * k:512 * k + 512], x_lo if l == 0 else evac_done, J_down(l - 1, N_GRP - 1) if l else 0, after_first=stats(2 * l))
                for kv in range(2):
                    def blk(k, kv=kv):
                        return BLK_t[:, 1920 * kv + 120 * k:1920 * kv + 120 * k + 120]
                    pe.wait_ge(sem("blk_lo"), 2 * l + kv + 1)
                    for n in range(2):
                        slab(n, J_cmp(l) + 2 * kv + n, 0, blk, None, 0, 60)
                nsa(l)
                retention(l)
                rwkv(l)
                need(pe, "w_lo", l)
                phase(J_out(l), N_OUT, lambda k: F0_t[:, 512 * k:512 * k + 512], None, 0)
                for g in range(N_GRP):
                    phase(J_up(l, g), 16, lambda k: F1_t[:, 512 * k:512 * k + 512], evac_done, J_out(l), after_first=stats(2 * l + 1) if g == 0 else None)
                    phase(J_down(l, g), 16, lambda k: U_t[:, 512 * k:512 * k + 512], evac_done, J_up(l, g))


def _pad(a, n):
    import numpy as np
    return np.concatenate([a, np.zeros(a.shape[:-1] + (n - a.shape[-1],), a.dtype)], -1)


def _constants():
    import numpy as np
    p = np.arange(128)
    c = {}
    c["ident"] = np.eye(128)
    c["one_d"] = np.full((128, 128), 1.0 / D)
    c["blk_sum"] = (p[:, None] // 64 == p[None, :] // 64).astype(float)
    c["blk_mean"] = c["blk_sum"] / 64
    c["one_h"] = np.full((128, 128), 1.0 / 128)

    def rot(h):
        m = np.zeros((128, 128))
        for j in range(128):
            if j % (2 * h) < h:
                m[j + h, j] = -1
            else:
                m[j - h, j] = 1
        return m

    def trig(h, pos):
        f = (np.float32(10000.0) ** (-np.arange(h, dtype=np.float32) / np.float32(h))).astype(np.float32)
        a = (pos.astype(np.float32)[None, :] * f[p % h][:, None]).astype(np.float32).astype(np.float64)
        return np.cos(a), np.sin(a)
    c["rot_r"], c["rot_n"] = rot(64), rot(32)
    t = np.arange(T)
    c["cos_r"], c["sin_r"] = trig(64, t)
    c["cos_n"], c["sin_n"] = trig(32, t)
    c["cos_c"], c["sin_c"] = trig(32, np.arange(16) * 16 + 31)
    lag = t[None, :] - p[:, None]
    c["decay"] = np.concatenate([np.where(lag >= 0, (1 - 2.0 ** (-5 - h)) ** np.maximum(lag, 0), 0.0) for h in range(4)], 1) * 128 ** -0.5
    c["causal"] = np.concatenate([np.zeros((128, 128)), np.where(p[None, :] <= p[:, None], 0.0, -1e30)], 1)
    n = np.arange(16)
    vis = np.concatenate([(16 * n[None, :] + 31 <= tt * 128 + p[:, None]) & (n[None, :] < 15) for tt in range(2)], 1)
    c["cmp_add"], c["cmp_vis"] = np.where(vis, 0.0, -1e30), vis.astype(float)
    same = p[:, None] // 64 == p[None, :] // 64
    c["rw_mask"] = np.concatenate([same & (p[:, None] < p[None, :]), same & (p[:, None] <= p[None, :])], 1).astype(float)
    c["lev"] = np.concatenate([((p[None, :] >> s) % 2 == 1) & ((p[:, None] >> s) == (p[None, :] >> s) - 1) for s in range(6)], 1).astype(float)
    c["scan"] = np.broadcast_to((t % 64 != 0).astype(float), (128, T))
    c["vcz"] = np.stack([(p // 32 == s // 2) & (p % 32 // 16 == s % 2) for s in range(8)], 1).astype(float)
    return np.concatenate([np.asarray(c[k], np.float32) for k in CON], 1)


def kernel(**inputs):
    import numpy as np
    import concourse.bacc as bacc
    from concourse.bass_utils import run_bass_kernel_spmd as run

    a = {k: np.asarray(v) for k, v in inputs.items()}
    heads = [8 * pg + 4 * h + q for pg in range(2) for q in range(4) for h in range(2)]
    hcols = np.concatenate([np.arange(64) + 64 * h for h in heads])

    def tiles(w):
        return w.reshape(16, 128, -1, 128).transpose(2, 1, 0, 3).reshape(-1, 128, 2048)

    slabs = np.empty((SLABS, 128, 2048), np.float32)
    vecs, small, cmpw = [], [], []
    o_rw, o_ns = 2048, 2048 + 1984

    def cols(v):
        return v.reshape(-1, 128).T

    for l in range(DEPTH):
        w = a["w_in"][l]
        vres = a["w_in_vres"][l - 1] if l else np.zeros((D, 64), np.float32)
        rw, ns = w[:, o_rw:o_ns], w[:, o_ns:]
        kv = [ns[:, 1024 + 256 * i:1280 + 256 * i] for i in range(6)]
        gates = ns[:, 2560:2608].reshape(D, 16, 3)[:, heads].reshape(D, 48)
        big = np.concatenate([rw[:, 0:1536], _pad(rw[:, 1536:1632], 128), _pad(rw[:, 1632:1728], 128), rw[:, 1728:1984],
                              _pad(np.concatenate([vres, gates], 1), 128), w[:, 0:2048], ns[:, hcols],
                              kv[2], kv[4], kv[0], kv[1], kv[3], kv[5]], 1)
        j = l * LAYER_SLABS
        slabs[j:j + N_IN] = tiles(big)
        j += N_IN
        slabs[j:j + 2] = tiles(a["nsa_cmp_k_w1"][l])
        slabs[j + 2:j + 4] = tiles(a["nsa_cmp_v_w1"][l])
        j += N_CMP
        wo = a["w_out"][l]
        slabs[j:j + N_OUT] = tiles(np.concatenate([wo[512:1024], wo[0:512], wo[1024:][hcols]]))
        j += N_OUT
        for g in range(N_GRP):
            slabs[j:j + 16] = tiles(a["w_up"][l][:, 2048 * g:2048 * g + 2048])
            slabs[j + 16:j + 32] = tiles(a["w_down"][l][2048 * g:2048 * g + 2048])
            j += 32
        mix = a["rwkv_mix"][l]
        vmix = a["rwkv_vres_mix"][l - 1] if l else np.zeros(64, np.float32)
        v0 = a["rwkv_v0"][l - 1] if l else np.zeros(512, np.float32)
        v2 = a["rwkv_v2"][l - 1] if l else np.zeros((64, 512), np.float32)
        mixes = np.concatenate([mix[0:1536], _pad(mix[1536:1632], 128), _pad(mix[1632:1728], 128), mix[1728:1984], _pad(vmix, 128)])

        def dup(v):
            return np.concatenate([v, v])[:, None]

        def rows(w):
            return _pad(w.T, 128).T

        kn = a["nsa_k_norm"][l]
        pe = [a["nsa_cmp_pe"][l, i].reshape(16, 128).T for i in range(2)]
        vecs.append(np.concatenate([cols(a["ln1_g"][l]), cols(a["ln2_g"][l]), cols(mixes), cols(a["rwkv_w0"][l]), cols(a["rwkv_a0"][l]),
                                    cols(v0), cols(a["rwkv_k_k"][l]), cols(a["rwkv_k_a"][l]), cols(a["rwkv_r_k"][l].reshape(-1)),
                                    cols(a["rwkv_ln_g"][l]), cols(a["rwkv_ln_b"][l]), dup(a["nsa_q_norm"][l]), dup(kn[0]), dup(kn[1]), dup(kn[2]),
                                    pe[0], pe[1]], 1))
        g2 = a["rwkv_g2"][l]
        small.append(np.concatenate([rows(a["rwkv_w2"][l]), rows(a["rwkv_a2"][l]), rows(v2), g2[0:128], g2[128:256]], 1))
        k2, w2 = a["nsa_cmp_k_w2"][l], a["nsa_cmp_v_w2"][l]
        cmpw.append(np.concatenate([k2[0:128], k2[0:128], k2[128:256], k2[128:256], w2[0:128], w2[128:256]], 1))

    x = np.ascontiguousarray(a["x"].reshape(T, 16, 128).transpose(2, 1, 0).reshape(128, 16 * T))
    arrays = {"slabs": slabs, "x": x, "vecs": np.ascontiguousarray(np.concatenate(vecs, 1)), "consts": np.ascontiguousarray(_constants()),
              "small": np.ascontiguousarray(np.stack(small)), "cmpw": np.ascontiguousarray(np.stack(cmpw))}
    nc = bacc.Bacc("TRN2", target_bir_lowering=False, num_devices=1)
    f32 = mybir.dt.float32
    args = [nc.dram_tensor(f"in_{k}", v.shape, f32, kind="ExternalInput").ap() for k, v in arrays.items()]
    out = nc.dram_tensor("out_t", (128, 16 * T), f32, kind="ExternalOutput").ap()
    v_first = nc.dram_tensor("v_first", (128, 4 * T), f32, kind="Internal").ap()
    hybrid_trunk(nc, *args, out, v_first)
    r = run(nc, [{f"in_{k}": v for k, v in arrays.items()}], core_ids=[0])
    got = np.asarray(r.results[0]["out_t"])
    return got.reshape(128, 16, T).transpose(2, 1, 0).reshape(1, T, D)
```

```python
import concourse.bass as bass
from concourse import mybir
from contextlib import ExitStack

D, T, DEPTH = 2048, 256, 2
KT = D // 128
N_IN, N_CMP, N_OUT, N_GRP = 53, 4, 16, 4
LAYER_SLABS = N_IN + N_CMP + N_OUT + N_GRP * 32
SLABS = DEPTH * LAYER_SLABS
RING = 4
HALF = KT // 2
RW_R, RW_K, RW_V, RW_W, RW_A, RW_G, RW_X = 0, 4, 8, 12, 13, 14, 16
RT_Q, RT_K, RT_V, RT_G = 17, 21, 25, 29
NS_Q, NS_KS, NS_KW, NS_KC, NS_VC, NS_VS, NS_VW = 33, 41, 43, 45, 47, 49, 51
M_RW, M_RT, M_NS = 0, 4, 8
VEC = {}
_at = 0
for _n, _w in [("g1", 16), ("g2", 16), ("mix", 17), ("w0", 4), ("a0", 4), ("v0", 4), ("kk", 4), ("ka", 4), ("rk", 4),
               ("lng", 4), ("lnb", 4), ("kn_c", 1), ("ng", 6), ("pe_k", 16), ("pe_v", 16)]:
    VEC[_n] = (_at, _at + _w)
    _at += _w
NVEC = _at
CON = {}
_at = 0
for _n, _w in [("ident", 128), ("one_d", 128), ("blk_mean", 128), ("blk_sum", 128), ("one_h", 128), ("rot_r", 128),
               ("rot_n", 128), ("cos_r", 256), ("sin_r", 256), ("cos_n", 256), ("sin_n", 256), ("cos_c", 16), ("sin_c", 16),
               ("decay", 1024), ("causal", 256), ("cmp_add", 32), ("cmp_vis", 32), ("rw_mask", 256), ("lev", 768),
               ("scan", 256), ("vcz", 8)]:
    CON[_n] = (_at, _at + _w)
    _at += _w
NCON = _at
LW = {"w2": (0, 512), "a2": (512, 1024), "v2": (1024, 1536), "g2": (1536, 2560)}
NLW = 2560
CW = {"k2": (0, 256), "v2": (256, 384)}
NCW = 384
KAPPA = 0.6065306597126334


def hybrid_trunk(nc, slabs, x_in, vecs, consts, small, cmpw, out, v_first, dbg=None):
    f32, f32r = mybir.dt.float32, mybir.dt.float32r
    ACT, ALU, AX = mybir.ActivationFunctionType, mybir.AluOpType, mybir.AxisListType
    ctx = ExitStack()
    with ctx:
        base = [16640]

        def place(name, cols, dt=f32, at=None):
            if at is None:
                at, base[0] = base[0], base[0] + (4 * cols + 31) // 32 * 32
            return nc.alloc_sbuf_tensor_at(name, [128, cols], dt, offset=at)

        X_t = place("x_res", KT * T)
        F0B = base[0]
        F0_t = place("act_f0", KT * 2 * T, f32r)
        RA = nc.alloc_sbuf_tensor_at("scratch_a", [128, 8192], f32, offset=F0B)
        PB = base[0]
        BLK_t = nc.alloc_sbuf_tensor_at("cmp_blocks", [128, 2 * 16 * 120], f32r, offset=PB)
        P_t = place("proj", N_IN * T)
        F1_t = place("act_f1", KT * 2 * T, f32r, PB)
        U_t = place("act_up", KT * 2 * T, f32r, PB + 32768)
        LW_t = place("lowrank_w", NLW, at=PB + N_IN * T * 4)
        base[0] = PB + 65536
        raw_t = place("raw", RING * KT * 128)
        RBB = base[0]
        hi_t = place("w_hi", 4 * HALF * 128, f32r)
        lo_t = place("w_lo", 4 * HALF * 128, f32r)
        RB = nc.alloc_sbuf_tensor_at("scratch_b", [128, 8192], f32, offset=RBB)
        bc_t = place("bcopy", 2 * T)
        s_t = place("evac_s", T)
        HVB = base[0]
        t_t = place("evac_t", T)
        sq_t = place("evac_sq", T)
        HV_t = nc.alloc_sbuf_tensor_at("cmp_v_hidden", [128, 2 * T], f32, offset=HVB)
        rstd_t = place("rstd", T)
        acc_t = place("sumsq", T)
        psq_t = place("psq", T)
        CM_t = place("consts_sb", NCON)
        VV_t = place("vecs_sb", DEPTH * NVEC)
        CW_t = place("cmp_w2", NCW)
        ST_t = place("state", 256)
        SN_t = place("state_new", 256)
        WC_t = place("chunk_decay", 16)
        EPS_t = place("eps", 8)
        KTC_t = place("k_cmp", 64)
        assert base[0] <= 229368, base[0]

        P = P_t[:, :].rearrange("p (k t) -> p k t", t=T)

        def con(name):
            return CM_t[:, CON[name][0]:CON[name][1]]

        def vec(l, name, i=0):
            c = l * NVEC + VEC[name][0] + i
            return VV_t[:, c:c + 1]

        def eps(i):
            return EPS_t[:, i:i + 1]
        E_RMS, E_KK, E_GN, E_LN8 = 0, 1, 2, 3

        PS_t = ctx.enter_context(nc.psum_tensor("banks", [128, 8, 512], f32))
        HID = P_t[:, NS_KC * T:(NS_KC + 4) * T]
        HT = HID[:, 512:1024]
        GL = SN_t[:, 0:96]
        SQ = P_t[:, RT_Q * T:RT_Q * T + 4 * T]
        DIF = P_t[:, NS_VS * T:NS_VS * T + 4 * T]
        PD = P_t[:, RT_Q * T:]
        VF_t = PD[:, 7168:8192]
        BD, TA, TB, PP, NM = RB[:, 4096:6144], RB[:, 0:1024], RB[:, 2048:3072], RB[:, 6144:7168], RB[:, 7168:8192]
        LBK = PD[:, 2048:6144]
        LB, LK = LBK[:, 0:2048], LBK[:, 2048:4096]
        PTB, CS, PC, MX, C1 = RB[:, 1536:2560], RB[:, 2560:3072], RB[:, 3072:3584], RB[:, 3584:3616], RB[:, 3616:3664]
        INN, RSQ, RO, RG = RB[:, 4096:5632], RB[:, 4096:5120], RB[:, 5632:6656], RB[:, 6656:7680]

        def SB(u):
            return RB[:, 512 * (u % 3):512 * (u % 3) + 512]
        UN = [(qt, tt, br) for qt in range(8) for tt in range(2) for br in range(2)]

        def bankc(j, w):
            return PS_t[:, j, 0:w]

        sems = {}

        def sem(name):
            if name not in sems:
                sems[name] = ctx.enter_context(nc.semaphore(name))
            return sems[name]

        raw_in = [sem(f"raw_in{i}") for i in range(RING)]
        x_in_s, con_in, vec_in = sem("x_in"), sem("con_in"), sem("vec_in")
        hi_ready, lo_ready, half_done = sem("hi_ready"), sem("lo_ready"), sem("half_done")
        bc_ready, sum_ready, evac_done = sem("bc_ready"), sem("sum_ready"), sem("evac_done")
        up_scaled, up_sq, u_hi = sem("up_scaled"), sem("up_sq"), sem("u_hi")
        x_upd, x_hi, x_lo, xg_ready = sem("x_upd"), sem("x_hi"), sem("x_lo"), sem("xg_ready")
        pool_sq, pool_acc = sem("pool_sq"), sem("pool_acc")
        stat_mm, stat_ln, rstd_ready = sem("stat_mm"), sem("stat_ln"), sem("rstd_ready")
        out_done, const_ready = sem("out_done"), sem("const_ready")
        dchain, achain = sem("dve_chain"), sem("act_chain")

        PER = dict(ks_ready=2, blk_sum=4, blk_hi=2, blk_lo=2, hid_ready=1, gelu_e=1, hv_ready=1, cmp_mm=1,
                   kc_sq=1, kc_ready=1, kc_mm=1, kc_rstd=1, kc_done=1,
                   nz=1, n_sq=3, n_mm=3, n_rstd=3, n_g=3, n_cos=3, n_sum=3, n_ln=3, n_rope=3, nv_t=1, nv_ev=1, ng_t=1, ng_e=1, ng_done=1,
                   cs_mm=2, cs_ready=2, cs_max=2, cs_exp=2, cs_p=2, cs_t=2, cs_ev=2,
                   s_mm=32, s_max=32, s_exp=32, s_p=32, p_t=32, p_ev=32, o_half=16, o_mm=16, o_hi=16, o_lo=16,
                   r_rot=2, r_cos=2, r_rope=2, r_vt=1, r_vev=1, r_in=4, r_dec=4, r_o=1, r_sq=1, r_mm=1, r_rstd=1, r_gate=1, r_out=1, r_fin=1, vc_out=1, r_hi=1, r_lo=1,
                   w_dif=5, w_mix=5, w_tw=1, w_sgx=1, w_xg=1, w_lr=1, w_e=1, w_sig=1, w_g=1, w_scan=1, w_pow=1, w_kk=1, w_kk2=1, w_kkmm=1,
                   w_kmax=1, w_krs=1, w_rk=1, w_bmm=1, w_bv=1, w_til=1, w_vt=1, w_vev=1, w_bz=1, w_bkt=2, w_bkev=2, w_bd=2,
                   w_l=4, w_lm=4, w_nm=24, w_am=4, w_ae=4, w_pm=20, w_pe=20, w_bm=20, w_be=20, w_xz=2,
                   w_x=4, w_xe=4, w_u=4, w_ue=4, w_s=4, w_se=4, w_y=2, w_ysum=2, w_ysq=2, w_yvar=2, w_yrs=2, w_yn=2, w_yt=2, w_yb=2, w_hi=2, w_lo=2)

        def up(ins, name):
            assert name in PER
            return ins.then_inc(sem(name), 1)

        def need(eng, name, l, k=None):
            eng.wait_ge(sem(name), (PER[name] if k is None else k) + l * PER[name])

        def J_in(l): return l * LAYER_SLABS
        def J_qk(l): return J_in(l) + 4
        def J_cmp(l): return J_qk(l) + 12
        def J_rw(l): return J_cmp(l) + N_CMP
        def J_rt(l): return J_rw(l) + 17
        def J_v(l): return J_rt(l) + 16
        def J_out(l): return J_in(l) + N_IN + N_CMP
        def J_up(l, g): return J_out(l) + N_OUT + 32 * g
        def J_down(l, g): return J_up(l, g) + 16

        def walk(eng, J0, count, body, peel=1):
            for n in range(peel):
                body(n, J0 + n, 0)
            loops = (count - peel) // 4
            if loops > 1:
                with eng.Fori(0, loops) as i:
                    for n in range(peel, peel + 4):
                        body(n, J0 + n, i)
            for n in range(peel + 4 * loops if loops > 1 else peel, count):
                body(n, J0 + n, 0)

        def at(i, c, k):
            return c if isinstance(i, int) else i * k + c

        def cols(t, i, c, k, w):
            return t[:, c:c + w] if isinstance(i, int) else t[:, bass.ds(i * k + c, w)]

        block = ctx.enter_context(nc.Block())

        @block.sync
        def _(sp):
            sp.dma_start(VV_t[:, :], vecs).then_inc(vec_in, 16)
            for q in range(4):
                sp.dma_start(X_t[:, q * 1024:(q + 1) * 1024], x_in[:, q * 1024:(q + 1) * 1024]).then_inc(x_in_s, 16)

            def load(s, i):
                dst = raw_t[:, (s % RING) * KT * 128:(s % RING + 1) * KT * 128]
                src = slabs[s, :, :] if isinstance(i, int) else slabs[bass.ds(i * 4 + s, 1), :, :].rearrange("a p n -> (a p) n")
                sp.dma_start(dst, src).then_inc(raw_in[s % RING], 16)

            load(0, 0)
            sp.dma_start(CM_t[:, :], consts).then_inc(con_in, 16)
            for s in range(1, RING):
                load(s, 0)
            loops = (SLABS - RING) // 4
            with sp.Fori(0, loops) as i:
                for s in range(RING):
                    sp.wait_ge(lo_ready, i * 8 + (2 * s + 2))
                    load(RING + s, i)
            for j in range(RING + loops * 4, SLABS):
                sp.wait_ge(lo_ready, 2 * (j - RING) + 2)
                load(j, 0)
            for q in range(4):
                sp.wait_ge(evac_done, J_down(DEPTH - 1, N_GRP - 1) + 4 * q + 4)
                sp.dma_start(out[:, q * 1024:(q + 1) * 1024], X_t[:, q * 1024:(q + 1) * 1024]).then_inc(out_done, 16)
            sp.wait_ge(out_done, 64)

        @block.gpsimd
        def _(pool):
            def square(k, n, i, first):
                x = X_t[:, bass.ds(i * T + n * T, T)] if not isinstance(i, int) else X_t[:, n * T:(n + 1) * T]
                pool.tensor_tensor(psq_t[:, :], x, x, ALU.mult).then_inc(pool_sq, 1)
                pool.wait_ge(pool_sq, i + (k + 1))
                if first:
                    pool.tensor_copy(acc_t[:, :], psq_t[:, :]).then_inc(pool_acc, 1)
                else:
                    pool.tensor_tensor(acc_t[:, :], acc_t[:, :], psq_t[:, :], ALU.add).then_inc(pool_acc, 1)
                pool.wait_ge(pool_acc, i + (k + 1))

            for nm in range(2 * DEPTH):
                if nm == 0:
                    pool.wait_ge(x_in_s, 64)
                else:
                    pool.wait_ge(x_upd, 16 * (nm - 1) + 1)
                    pool.wait_ge(stat_mm, nm)
                square(16 * nm, 0, 0, True)
                with pool.Fori(0, 15) as i:
                    if nm:
                        pool.wait_ge(x_upd, i + (16 * (nm - 1) + 2))
                    square(16 * nm + 1, 1, i, False)

        @block.scalar
        def _(act):
            acount = [0]

            def link(ins):
                acount[0] += 1
                ins.then_inc(achain, 1)
                act.wait_ge(achain, acount[0])

            def split_hi(s, i):
                act.wait_ge(raw_in[s % RING], i * 16 + 16 * (s // RING + 1))
                for a in range(2):
                    h = 2 * s + a
                    if h >= 4:
                        act.wait_ge(half_done, i * 8 + (h - 3))
                    act.activation(hi_t[:, (h % 4) * 1024:(h % 4) * 1024 + 1024],
                                   raw_t[:, (s % RING) * 2048 + a * 1024:(s % RING) * 2048 + a * 1024 + 1024],
                                   ACT.Copy).then_inc(hi_ready, 1)

            def phase(J0, count, evac_hi, w=T, ahead=0, peel=1, aux=None):
                def body(n, s, i):
                    if s + 2 < SLABS and n < count - ahead:
                        split_hi(s + 2, i)
                    act.wait_ge(half_done, i * 8 + (2 * s + 2))
                    if s >= 2:
                        act.wait_ge(sum_ready, i * 4 + (s - 1))
                    act.activation(bc_t[:, (s % 2) * T:(s % 2) * T + w], PS_t[:, s % RING, w:2 * w], ACT.Copy).then_inc(bc_ready, 1)
                    if evac_hi:
                        evac_hi(n, i)
                    if aux:
                        aux(n - peel, i)
                walk(act, J0, count, body, peel)

            def dyn(t, c, k, i, w):
                return t[:, c:c + w] if isinstance(i, int) else t[:, bass.ds(i * k + c, w)]

            def x_hi_step(nm, l, gname, dst):
                def f(n, i):
                    act.wait_ge(xg_ready, i * 4 + (16 * (nm - 1) + n + 1))
                    act.activation(dyn(dst, n * 512, 2048, i, 256), t_t[:, :], ACT.Copy).then_inc(x_hi, 1)
                return f

            def u_hi_step(l, g):
                def f(n, i):
                    act.wait_ge(up_sq, i * 4 + (64 * l + 16 * g + n + 1))
                    act.activation(dyn(U_t, n * 512, 2048, i, 256), sq_t[:, :], ACT.Copy).then_inc(u_hi, 1)
                return f

            def stats(nm):
                act.wait_ge(stat_mm, nm + 1)
                act.activation(rstd_t[:, :], PS_t[:, 4, 0:T], ACT.Ln, bias=eps(E_RMS)).then_inc(stat_ln, 1)
                act.wait_ge(stat_ln, nm + 1)
                act.activation(rstd_t[:, :], rstd_t[:, :], ACT.Exp, scale=-0.5).then_inc(rstd_ready, 1)

            def blocks(l):
                def aux(n, i):
                    if n == 3:
                        need(act, "blk_sum", l, i * 2 + 2)
                        up(act.activation(cols(BLK_t, i, 0, 1920, 1920).rearrange("p (r c) -> p r c", c=120)[:, :, 0:60],
                                          cols(P_t, i, (RT_Q + 8) * T, 1024, 960).rearrange("p (r c) -> p r c", c=60), ACT.Copy), "blk_hi")
                return aux

            def norms(l):
                def aux(n, i):
                    if n == 0:
                        need(act, "n_rope", l, i + 0)
                        up(act.activation(SQ, cols(P_t, i, NS_Q * T, 1024, 1024), ACT.Square), "n_sq")
                    if n == 2:
                        need(act, "n_mm", l, i + 1)
                        for b in range(2):
                            ins = act.activation(SQ[:, 512 * b:512 * b + 512], bankc(4 + b, 512), ACT.Ln, bias=eps(E_RMS))
                        link_loop(ins, l, i)
                        up(act.activation(SQ, SQ, ACT.Exp, scale=-0.5, bias=cols(EPS_t, i, E_LN8, 1, 1)), "n_rstd")
                return aux

            def link_loop(ins, l, i):
                up(ins, "n_ln")
                need(act, "n_ln", l, i + 1)

            def gelu(l):
                def aux(n, i):
                    if n == 1:
                        need(act, "hid_ready", l)
                        up(act.activation(HT[:, 256:496], HT[:, 256:496], ACT.Exp, scale=-1.5957691216057308), "gelu_e")
                return aux

            def compress(l):
                def aux(n, i):
                    if n == 0:
                        need(act, "cmp_mm", l)
                        up(act.activation(HT[:, 0:60], PS_t[:, 4, 0:60], ACT.Square), "kc_sq")
                    if n == 1:
                        need(act, "kc_mm", l)
                        link(act.activation(HT[:, 0:60], PS_t[:, 4, 64:124], ACT.Ln, bias=eps(E_RMS)))
                        up(act.activation(HT[:, 0:60], HT[:, 0:60], ACT.Exp, scale=-0.5), "kc_rstd")
                        need(act, "ng_t", l)
                        up(act.activation(GL.rearrange("p (a g) -> p a g", g=48), PS_t[:, 6, 0:256].rearrange("p (a c) -> p a c", c=128)[:, :, 64:112],
                                          ACT.Exp, scale=-1.0), "ng_e")
                    if n == 2:
                        need(act, "r_vt", l)
                        for tt in range(2):
                            ins = act.activation(P_t[:, RT_V * T + 512 * tt:RT_V * T + 512 * tt + 512], bankc(5 + 2 * tt, 512), ACT.Copy)
                        up(ins, "r_vev")
                return aux

            def nsa(l):
                act.wait_ge(half_done, 2 * J_out(l))
                up(act.activation(RG, P_t[:, RT_G * T:(RT_G + 4) * T], ACT.Exp, scale=-1.0), "r_gate")
                need(act, "nv_t", l)
                for tt in range(2):
                    ins = act.activation(P_t[:, NS_VS * T + 512 * tt:NS_VS * T + 512 * tt + 512], bankc(2 + tt, 512), ACT.Copy)
                up(ins, "nv_ev")
                for tt in range(2):
                    need(act, "cs_max", l, tt + 1)
                    up(act.activation(CS[:, 256 * tt:256 * tt + 256], CS[:, 256 * tt:256 * tt + 256], ACT.Exp), "cs_exp")
                need(act, "r_o", l)
                for b in range(2):
                    ins = act.activation(RSQ[:, 512 * b:512 * b + 512], bankc(4 + b, 512), ACT.Square)
                up(ins, "r_sq")
                for tt in range(2):
                    need(act, "cs_t", l, tt + 1)
                    up(act.activation(PC[:, 256 * tt:256 * tt + 256], PS_t[:, 6 + tt, 0:256], ACT.Copy), "cs_ev")
                need(act, "r_mm", l)
                for b in range(2):
                    ins = act.activation(RSQ[:, 512 * b:512 * b + 512], bankc(2 + b, 512), ACT.Ln, bias=eps(E_RMS))
                link(ins)
                up(act.activation(RSQ, RSQ, ACT.Exp, scale=-0.5), "r_rstd")

                def exps(u):
                    tt, w = UN[u][1], 128 * (UN[u][1] + 1)
                    need(act, "s_max", l, u + 1)
                    S = SB(u)
                    mx = MX[:, 8 * (u % 4):8 * (u % 4) + 8]
                    for h in range(2):
                        ins = act.activation(S[:, h * w:(h + 1) * w], S[:, h * w:(h + 1) * w], ACT.Exp, bias=mx[:, h:h + 1],
                                             accum_out=mx[:, 2 + h:3 + h])
                    up(ins, "s_exp")

                def evac(u):
                    tt = UN[u][1]
                    need(act, "p_t", l, u + 1)
                    if u >= 2:
                        need(act, "o_mm" if u % 2 else "o_half", l, u // 2)
                    n = 256 * (tt + 1)
                    up(act.activation(PTB[:, 512 * (u % 2):512 * (u % 2) + n], PS_t[:, 2 + u % 2, 0:n], ACT.Copy), "p_ev")

                def ohi(v):
                    qt, tt = v // 2, v % 2
                    need(act, "o_mm", l, v + 1)
                    up(act.activation(F0_t[:, (M_NS + qt) * 512 + tt * 128:(M_NS + qt) * 512 + tt * 128 + 128],
                                      PS_t[:, 4 + v % 2, 0:128], ACT.Copy), "o_hi")

                for u in range(32 + 2):
                    if u < 32:
                        exps(u)
                    if u == 1:
                        need(act, "r_fin", l)
                        F = F0_t[:, M_RT * 512:(M_RT + 4) * 512].rearrange("p (k c) -> p k c", c=512)
                        up(act.activation(F[:, :, 0:256], RO.rearrange("p (k t) -> p k t", t=256), ACT.Copy), "r_hi")
                    if u >= 1 and u - 1 < 32:
                        evac(u - 1)
                    if u >= 2 and (u - 2) % 2 == 1:
                        ohi((u - 2) // 2)

            def rwkv(l):
                need(act, "w_mix", l)
                if l == 0:
                    act.dma_start(v_first, P_t[:, RW_V * T:(RW_V + 4) * T]).then_inc(sem("vf_out"), 16)
                else:
                    act.dma_start(VF_t, v_first).then_inc(sem("vf_in"), 16)
                up(act.activation(P[:, RW_W, :], P[:, RW_W, :], ACT.Tanh), "w_tw")
                up(act.activation(P_t[:, RW_G * T:(RW_G + 2) * T], P_t[:, RW_G * T:(RW_G + 2) * T], ACT.Sigmoid), "w_xg")
                need(act, "w_lr", l)
                for b, (dst, bias) in enumerate([(0, "w0"), (1024, "a0"), (2048, "v0")][:3 if l else 2]):
                    for c in range(4):
                        ins = act.activation(RB[:, dst + 256 * c:dst + 256 * c + 256], PS_t[:, 2 * b + c // 2, (c % 2) * 256:(c % 2) * 256 + 256],
                                             ACT.Sigmoid, bias=vec(l, bias, c))
                up(ins, "w_e")
                for b in range(2):
                    ins = act.activation(PD[:, 512 * b:512 * b + 512], bankc(6 + b, 512), ACT.Copy)
                up(ins, "w_g")
                need(act, "w_scan", l)
                act.activation(PD[:, 3072:4096], PD[:, 2048:3072], ACT.Exp, scale=-KAPPA)
                act.activation(PD[:, 4096:5120], PD[:, 2048:3072], ACT.Exp, scale=KAPPA)
                up(act.activation(PD[:, 5120:6144], RB[:, 0:1024], ACT.Exp, scale=-KAPPA), "w_pow")
                need(act, "w_kk", l)
                up(act.activation(RB[:, 4096:5120], RB[:, 3072:4096], ACT.Square), "w_kk2")
                need(act, "w_kmax", l)
                link(act.activation(RB[:, 4096:5120], RB[:, 4096:5120], ACT.Ln, scale=65536.0))
                up(act.activation(RB[:, 4096:5120], RB[:, 4096:5120], ACT.Exp, scale=-0.5, bias=eps(E_KK)), "w_krs")
                need(act, "w_vt", l)
                for tt in range(2):
                    ins = act.activation(P_t[:, RW_W * T + 512 * tt:RW_W * T + 512 * tt + 512], bankc(tt, 512), ACT.Copy)
                up(ins, "w_vev")
                act.wait_ge(sem("vf_out"), 16)
                for tt in range(2):
                    need(act, "w_bkt", l, tt + 1)
                    for q in range(2):
                        ins = act.activation(P_t[:, RW_V * T + 512 * q:RW_V * T + 512 * q + 512], bankc(2 + q, 512), ACT.Copy)
                    up(ins, "w_bkev")
                    for s in range(1, 6):
                        for q in range(2):
                            need(act, "w_pm", l, 10 * tt + 2 * (s - 1) + q + 1)
                            up(act.activation(RB[:, 6144 + 512 * q:6656 + 512 * q], bankc(q, 512), ACT.Copy), "w_pe")
                    for c in range(2):
                        r = slice(64 * c, 64 * c + 64)
                        ch = 2 * tt + c
                        need(act, "w_x", l, ch + 1)
                        up(act.activation(RB[r, 0:512], PS_t[r, 0, :], ACT.Copy), "w_xe")
                        need(act, "w_u", l, ch + 1)
                        up(act.activation(RB[r, 512:1024], PS_t[r, 1, :], ACT.Copy), "w_ue")
                    need(act, "w_ysum", l, tt + 1)
                    up(act.activation(RB[:, 6656:7168], RB[:, 6144:6656], ACT.Square), "w_ysq")
                    need(act, "w_yvar", l, tt + 1)
                    link(act.activation(RB[:, 7184:7192], RB[:, 7176:7184], ACT.Ln, scale=1.0 / 64, bias=eps(E_GN)))
                    up(act.activation(RB[:, 7184:7192], RB[:, 7184:7192], ACT.Exp, scale=-0.5), "w_yrs")
                    need(act, "w_yb", l, tt + 1)
                    F = F0_t[:, M_RW * 512:(M_RW + 4) * 512].rearrange("p (k c) -> p k c", c=512)
                    up(act.activation(F[:, :, tt * 128:tt * 128 + 128], RB[:, 6144:6656].rearrange("p (k t) -> p k t", t=128), ACT.Copy), "w_hi")

            act.wait_ge(vec_in, 16)
            act.wait_ge(x_in_s, 64)
            for n in range(KT):
                act.activation(F0_t[:, n * 512:n * 512 + 256], X_t[:, n * T:(n + 1) * T], ACT.Copy, scale=vec(0, "g1", n)).then_inc(x_hi, 1)
            split_hi(0, 0)
            split_hi(1, 0)
            act.wait_ge(const_ready, 1)
            for l in range(DEPTH):
                if l:
                    act.wait_ge(half_done, 2 * J_in(l))
                act.dma_start(LW_t[:, :], small[l, :, :]).then_inc(sem("small_in"), 16)
                act.dma_start(CW_t[:, :], cmpw[l, :, :]).then_inc(sem("cw_in"), 16)
                stats(2 * l)
                phase(J_in(l), 4, None)
                phase(J_qk(l), 8, None, peel=0, aux=blocks(l))
                phase(J_qk(l) + 8, 4, None)
                phase(J_cmp(l), N_CMP, None, w=60)
                phase(J_rw(l), 13, None, aux=norms(l))
                phase(J_rw(l) + 13, 4, None, peel=0, aux=gelu(l))
                phase(J_rt(l), 16, None, peel=0)
                phase(J_v(l), 4, None, peel=0, ahead=2, aux=compress(l))
                nsa(l)
                rwkv(l)
                need(act, "w_lo", l)
                split_hi(J_out(l), 0)
                split_hi(J_out(l) + 1, 0)
                phase(J_out(l), N_OUT, x_hi_step(2 * l + 1, l, "g2", F1_t))
                stats(2 * l + 1)
                for g in range(N_GRP):
                    phase(J_up(l, g), 16, u_hi_step(l, g))
                    norm = g == N_GRP - 1 and l + 1 < DEPTH
                    phase(J_down(l, g), 16, x_hi_step(2 * l + 2, l + 1, "g1", F0_t) if norm else None)

        @block.vector
        def _(dve):
            dcount = [0]

            def link(ins):
                dcount[0] += 1
                ins.then_inc(dchain, 1)
                dve.wait_ge(dchain, dcount[0])

            def split_lo(s, i, a):
                h = 2 * s + a
                dve.wait_ge(hi_ready, i * 8 + (h + 1))
                c = (h % 4) * 1024
                dve.tensor_tensor(lo_t[:, c:c + 1024], raw_t[:, (s % RING) * 2048 + a * 1024:(s % RING) * 2048 + a * 1024 + 1024],
                                  hi_t[:, c:c + 1024].bitcast(f32), ALU.subtract).then_inc(lo_ready, 1)

            def dyn(t, c, k, i, w):
                return t[:, c:c + w] if isinstance(i, int) else t[:, bass.ds(i * k + c, w)]

            def phase(J0, count, evac, w=T, ahead=0, peel=1, aux=None):
                def body(n, s, i):
                    split = s + 2 < SLABS and n < count - ahead
                    if split:
                        split_lo(s + 2, i, 0)
                    dve.wait_ge(bc_ready, i * 4 + (s + 1))
                    if s:
                        dve.wait_ge(evac_done, i * 4 + s)
                    dve.tensor_tensor(s_t[:, 0:w], PS_t[:, s % RING, 0:w], bc_t[:, (s % 2) * T:(s % 2) * T + w], ALU.add).then_inc(sum_ready, 1)
                    if split:
                        split_lo(s + 2, i, 1)
                    dve.wait_ge(sum_ready, i * 4 + (s + 1))
                    evac(n, i)
                    if aux:
                        aux(n - peel, i)
                walk(dve, J0, count, body, peel)

            def proj_evac(tile):
                def f(n, i):
                    dve.tensor_tensor(dyn(P_t, (tile + n) * T, 4 * T, i, T), s_t[:, :], rstd_t[:, :], ALU.mult).then_inc(evac_done, 1)
                return f

            def cmp_evac(l):
                def f(n, i):
                    dve.tensor_copy(HID[:, 60 * n:60 * n + 60], s_t[:, 0:60]).then_inc(evac_done, 1)
                return f

            def up_evac(l, g):
                def f(n, i):
                    u = 64 * l + 16 * g + n
                    dve.tensor_tensor(t_t[:, :], s_t[:, :], rstd_t[:, :], ALU.mult).then_inc(up_scaled, 1)
                    dve.wait_ge(up_scaled, i * 4 + (u + 1))
                    dve.scalar_tensor_tensor(out=sq_t[:, :], in0=t_t[:, :], scalar=0.0, in1=t_t[:, :], op0=ALU.max, op1=ALU.mult).then_inc(up_sq, 1)
                    dve.wait_ge(u_hi, i * 4 + (u + 1))
                    dve.tensor_tensor(dyn(U_t, n * 512 + 256, 2048, i, 256), sq_t[:, :], dyn(U_t, n * 512, 2048, i, 256).bitcast(f32),
                                      ALU.subtract).then_inc(evac_done, 1)
                return f

            def x_evac(nm, l, gname, dst, norm):
                def f(n, i):
                    k = 16 * (nm - 1) + n if nm else 0
                    ins = dve.tensor_tensor(dyn(X_t, n * T, 4 * T, i, T), s_t[:, :], dyn(X_t, n * T, 4 * T, i, T), ALU.add)
                    ins.then_inc(x_upd if norm else evac_done, 1)
                    if norm:
                        dve.wait_ge(x_upd, i * 4 + (k + 1))
                        g0 = l * NVEC + VEC[gname][0]
                        dve.tensor_scalar(t_t[:, :], dyn(X_t, n * T, 4 * T, i, T), dyn(VV_t, g0 + n, 4, i, 1), None, ALU.mult).then_inc(xg_ready, 1)
                        dve.wait_ge(x_hi, i * 4 + (k + 17))
                        dve.tensor_tensor(dyn(dst, n * 512 + 256, 2048, i, 256), t_t[:, :], dyn(dst, n * 512, 2048, i, 256).bitcast(f32),
                                          ALU.subtract).then_inc(evac_done, 1)
                return f

            def blocks(l):
                def aux(n, i):
                    K = cols(P_t, i, RT_Q * T, 1024, 1024).rearrange("p (g t) -> p g t", t=T)
                    V = K.rearrange("p g (n r) -> p r g n", r=16)
                    O = cols(P_t, i, (RT_Q + 8) * T, 1024, 960).rearrange("p (r g n) -> p r g n", g=4, n=15)
                    if n == 0:
                        for g in range(4):
                            r = slice(64 * (g % 2), 64 * (g % 2) + 64)
                            src = cols(P_t[r, :], i, (NS_KC + g // 2) * T, 2 * T, T)
                            dve.tensor_copy(K[0:64, g, :], src)
                            ins = dve.tensor_copy(K[64:128, g, 0:255], src[:, 1:256])
                        up(ins, "ks_ready")
                    if n in (1, 2):
                        if n == 1:
                            need(dve, "ks_ready", l, i + 1)
                        half = n - 1
                        pe = cols(VV_t, i, l * NVEC + VEC["pe_k"][0], 16, 16)
                        for g in range(4):
                            ins = dve.tensor_tensor(O[:, 8 * half:8 * half + 8, g, :], V[:, 0:16:2, g, half:half + 15],
                                                    pe[:, 8 * half:8 * half + 8].unsqueeze(2).to_broadcast([128, 8, 15]), ALU.add)
                        up(ins, "blk_sum")
                    if n == 3:
                        need(dve, "blk_hi", l, i + 1)
                        B = cols(BLK_t, i, 0, 1920, 1920).rearrange("p (r c) -> p r c", c=120)
                        up(dve.tensor_tensor(B[:, :, 60:120], cols(P_t, i, (RT_Q + 8) * T, 1024, 960).rearrange("p (r c) -> p r c", c=60),
                                             B[:, :, 0:60].bitcast(f32), ALU.subtract), "blk_lo")
                return aux

            def norms(l):
                def aux(n, i):
                    Q4 = cols(P_t, i, NS_Q * T, 1024, 1024)
                    Q43 = Q4.rearrange("p (a t) -> p a t", t=T)
                    if n == 0:
                        need(dve, "n_sq", l, i + 1)
                        for b in range(2):
                            ins = dve.tensor_scalar(Q4[:, 512 * b:512 * b + 512], Q4[:, 512 * b:512 * b + 512],
                                                    cols(VV_t, i, l * NVEC + VEC["ng"][0] + b, 2, 1), None, ALU.mult)
                        up(ins, "n_g")
                    if n == 2:
                        need(dve, "n_mm", l, i + 1)
                        for b in range(2):
                            R3 = bankc(6 + b, 512).rearrange("p (a t) -> p a t", t=T)
                            dve.tensor_tensor(R3, R3, con("sin_n").unsqueeze(1).to_broadcast([128, 2, 256]), ALU.mult)
                        up(dve.tensor_tensor(Q43, Q43, con("cos_n").unsqueeze(1).to_broadcast([128, 4, 256]), ALU.mult), "n_cos")
                    if n == 3:
                        need(dve, "n_cos", l, i + 1)
                        for b in range(2):
                            ins = dve.tensor_tensor(Q4[:, 512 * b:512 * b + 512], Q4[:, 512 * b:512 * b + 512], bankc(6 + b, 512), ALU.add)
                        up(ins, "n_sum")
                        need(dve, "n_sum", l, i + 1)
                        need(dve, "n_rstd", l, i + 1)
                        up(dve.tensor_tensor(Q4, Q4, SQ, ALU.mult), "n_rope")
                return aux

            def gelu(l):
                H = HID[:, 0:240]

                def aux(n, i):
                    if n == 0:
                        link(dve.tensor_tensor(HT[:, 0:240], H, H, ALU.mult))
                        link(dve.tensor_scalar(HT[:, 0:240], HT[:, 0:240], 0.044715, 1.0, ALU.mult, ALU.add))
                        up(dve.tensor_tensor(HT[:, 256:496], HT[:, 0:240], H, ALU.mult), "hid_ready")
                    if n == 2:
                        need(dve, "gelu_e", l)
                        link(dve.tensor_scalar(HT[:, 256:496], HT[:, 256:496], 1.0, None, ALU.add))
                        link(dve.reciprocal(HT[:, 256:496], HT[:, 256:496]))
                        link(dve.tensor_tensor(HID[:, 256:496], H, HT[:, 256:496], ALU.mult))
                        link(dve.memset(HV_t[:, :], 0.0))
                    if n == 3:
                        for ht in range(2):
                            for pg in range(2):
                                src = HID[:, 256 + 120 + 60 * ht + 30 * pg:256 + 120 + 60 * ht + 30 * pg + 30].rearrange("p (h n) -> p h n", n=15)
                                ins = dve.tensor_copy(HV_t[:, ht * 256 + pg * 128:ht * 256 + pg * 128 + 128].rearrange("p (q h n) -> p q h n", q=4, h=2)[:, :, :, 0:15],
                                                      src.unsqueeze(1).to_broadcast([128, 4, 2, 15]))
                        up(ins, "hv_ready")
                return aux

            def shift(l, half):
                def aux(n, i):
                    c = 4 * T * 2 * half
                    P3 = cols(P_t, i, c, 1024, 1024).rearrange("p (a t) -> p a t", t=T)
                    D3 = DIF.rearrange("p (a t) -> p a t", t=T)
                    if n == 0:
                        need(dve, "w_mix", l, i + 2 * half)
                        dve.tensor_tensor(D3[:, :, 1:T], P3[:, :, 0:T - 1], P3[:, :, 1:T], ALU.subtract)
                        up(dve.tensor_scalar(D3[:, :, 0:1], P3[:, :, 0:1], -1.0, None, ALU.mult), "w_dif")
                    if n == 1:
                        need(dve, "w_dif", l, i + (2 * half + 1))
                        for a in range(4):
                            ins = dve.scalar_tensor_tensor(out=P3[:, a, :], in0=D3[:, a, :], scalar=cols(VV_t, i, l * NVEC + VEC["mix"][0] + 8 * half + a, 4, 1),
                                                           in1=P3[:, a, :], op0=ALU.mult, op1=ALU.add)
                        up(ins, "w_mix")
                    if half:
                        R4 = cols(P_t, i, RT_Q * T, 1024, 1024)
                        R43 = R4.rearrange("p (a t) -> p a t", t=T)
                        if n == 2:
                            need(dve, "r_rot", l, i + 1)
                            for b in range(2):
                                R3 = bankc(4 + b, 512).rearrange("p (a t) -> p a t", t=T)
                                dve.tensor_tensor(R3, R3, con("sin_r").unsqueeze(1).to_broadcast([128, 2, 256]), ALU.mult)
                            up(dve.tensor_tensor(R43, R43, con("cos_r").unsqueeze(1).to_broadcast([128, 4, 256]), ALU.mult), "r_cos")
                        if n == 3:
                            need(dve, "r_cos", l, i + 1)
                            for b in range(2):
                                ins = dve.tensor_tensor(R4[:, 512 * b:512 * b + 512], R4[:, 512 * b:512 * b + 512], bankc(4 + b, 512), ALU.add)
                            up(ins, "r_rope")
                return aux

            def compress(l):
                def g4(ap):
                    return ap.rearrange("p (g n) -> p g n", n=15)

                def aux(n, i):
                    if n == 0:
                        X1 = P[:, RW_X, :]
                        dve.tensor_tensor(psq_t[:, 1:T], X1[:, 0:T - 1], X1[:, 1:T], ALU.subtract)
                        up(dve.tensor_scalar(psq_t[:, 0:1], X1[:, 0:1], -1.0, None, ALU.mult), "w_dif")
                        need(dve, "w_dif", l)
                        up(dve.scalar_tensor_tensor(out=X1, in0=psq_t[:, :], scalar=vec(l, "mix", 16), in1=X1, op0=ALU.mult, op1=ALU.add), "w_mix")
                        need(dve, "kc_sq", l)
                        dve.tensor_scalar(HT[:, 64:124], PS_t[:, 4, 0:60], vec(l, "kn_c"), None, ALU.mult)
                        link(dve.tensor_copy(HT[:, 256:384], PS_t[:, 4, 256:384]))
                        up(dve.memset(KTC_t[:, :], 0.0), "kc_ready")
                    if n == 2:
                        need(dve, "kc_ready", l)
                        need(dve, "kc_mm", l)
                        need(dve, "kc_rstd", l)
                        cosb = con("cos_c")[:, 0:15].unsqueeze(1).to_broadcast([128, 4, 15])
                        sinb = con("sin_c")[:, 0:15].unsqueeze(1).to_broadcast([128, 4, 15])
                        dve.tensor_tensor(g4(HT[:, 128:188]), g4(HT[:, 64:124]), cosb, ALU.mult)
                        link(dve.tensor_tensor(g4(HT[:, 192:252]), g4(PS_t[:, 4, 128:188]), sinb, ALU.mult))
                        link(dve.tensor_tensor(HT[:, 128:188], HT[:, 128:188], HT[:, 192:252], ALU.add))
                        KC = KTC_t[:, :].rearrange("p (a h n) -> p a h n", h=2, n=16)
                        for h in range(2):
                            r = slice(64 * h, 64 * h + 64)
                            a = HT[r, 128:188].rearrange("p (a h n) -> p a h n", h=2, n=15)[:, :, h, :]
                            b = HT[r, 0:60].rearrange("p (a h n) -> p a h n", h=2, n=15)[:, :, h, :]
                            ins = dve.tensor_tensor(KC[r, :, h, 0:15], a, b, ALU.mult)
                        up(ins, "kc_done")
                        need(dve, "ng_e", l)
                        link(dve.tensor_scalar(GL, GL, 1.0, None, ALU.add))
                        up(dve.reciprocal(GL, GL), "ng_done")
                return aux

            def nsa(l):
                dve.wait_ge(half_done, 2 * J_out(l))
                for h in range(4):
                    need(dve, "r_in", l, h + 1)
                    dec = con("decay")[:, 256 * h:256 * h + 256]
                    dve.tensor_tensor(INN[:, 384 * h:384 * h + 256], PS_t[:, 4 + h, 0:256], dec, ALU.mult)
                    up(dve.tensor_tensor(INN[:, 384 * h + 256:384 * h + 384], PS_t[:, 4 + h, 256:384], dec[:, 0:128], ALU.mult), "r_dec")
                need(dve, "ng_done", l)
                GV = GL.rearrange("p (a h b) -> p a h b", h=16, b=3)
                for tt in range(2):
                    if tt:
                        need(dve, "cs_max", l, tt)
                    need(dve, "cs_mm", l, tt + 1)
                    C = CS[:, 256 * tt:256 * tt + 256]
                    C3 = C.rearrange("p (h n) -> p h n", n=16)
                    m = con("cmp_add")[:, 16 * tt:16 * tt + 16].unsqueeze(1).to_broadcast([128, 16, 16])
                    link(dve.tensor_tensor(C3, PS_t[:, tt, 0:256].rearrange("p (h n) -> p h n", n=16), m, ALU.add))
                    link(dve.tensor_reduce(C1[:, 0:16], C3, AX.X, ALU.max))
                    up(dve.tensor_tensor(C3, C3, C1[:, 0:16].unsqueeze(2).to_broadcast([128, 16, 16]), ALU.subtract), "cs_max")
                VZ = RA[:, 512:1536]
                for pg in range(2):
                    ins = dve.tensor_tensor(VZ[:, pg * 512:(pg + 1) * 512].rearrange("p (s d) -> p s d", d=64),
                                            HT[:, 256 + 64 * pg:320 + 64 * pg].unsqueeze(1).to_broadcast([128, 8, 64]),
                                            con("vcz").unsqueeze(2).to_broadcast([128, 8, 64]), ALU.mult)
                up(ins, "nz")
                need(dve, "cs_max", l)
                for tt in range(2):
                    if tt:
                        need(dve, "cs_p", l, tt)
                    need(dve, "cs_exp", l, tt + 1)
                    C3 = CS[:, 256 * tt:256 * tt + 256].rearrange("p (h n) -> p h n", n=16)
                    vis = con("cmp_vis")[:, 16 * tt:16 * tt + 16].unsqueeze(1).to_broadcast([128, 16, 16])
                    link(dve.tensor_reduce(C1[:, 0:16], C3[:, :, 0:15], AX.X, ALU.add))
                    link(dve.reciprocal(C1[:, 16:32], C1[:, 0:16]))
                    link(dve.tensor_tensor(C1[:, 32:48], C1[:, 16:32], GV[:, tt, :, 0], ALU.mult))
                    link(dve.tensor_tensor(C3, C3, vis, ALU.mult))
                    up(dve.tensor_tensor(C3, C3, C1[:, 32:48].unsqueeze(2).to_broadcast([128, 16, 16]), ALU.mult), "cs_p")

                def maxes(u):
                    qt, tt, br = UN[u]
                    w = 128 * (tt + 1)
                    need(dve, "s_mm", l, u + 1)
                    if u >= 3:
                        need(dve, "p_t", l, u - 2)
                    S = SB(u)
                    mx = MX[:, 8 * (u % 4):8 * (u % 4) + 8]
                    mask = con("causal")[:, 128 * (1 - tt):256]
                    for h in range(2):
                        ins = dve.tensor_tensor_reduce(S[:, h * w:(h + 1) * w], PS_t[:, u % 2 + 6 * h, 0:w], mask, 1.0, -3.0e38,
                                                       ALU.add, ALU.max, mx[:, 4 + h:5 + h])
                    link(ins)
                    up(dve.tensor_scalar(mx[:, 0:2], mx[:, 4:6], -1.0, None, ALU.mult), "s_max")

                def probs(u):
                    qt, tt, br = UN[u]
                    w = 128 * (tt + 1)
                    need(dve, "s_exp", l, u + 1)
                    S = SB(u)
                    mx = MX[:, 8 * (u % 4):8 * (u % 4) + 8]
                    link(dve.reciprocal(mx[:, 6:8], mx[:, 2:4]))
                    link(dve.tensor_tensor(mx[:, 6:8], mx[:, 6:8], GV[:, tt, 2 * qt:2 * qt + 2, 1 + br], ALU.mult))
                    for h in range(2):
                        ins = dve.tensor_scalar(S[:, h * w:(h + 1) * w], S[:, h * w:(h + 1) * w], mx[:, 6 + h:7 + h], None, ALU.mult)
                    up(ins, "s_p")

                def olo(v):
                    qt, tt = v // 2, v % 2
                    need(dve, "o_hi", l, v + 1)
                    c = (M_NS + qt) * 512 + tt * 128
                    up(dve.tensor_tensor(F0_t[:, c + 256:c + 384], PS_t[:, 4 + v % 2, 0:128], F0_t[:, c:c + 128].bitcast(f32), ALU.subtract), "o_lo")

                need(dve, "r_gate", l)
                link(dve.tensor_scalar(RG, RG, 1.0, None, ALU.add))
                link(dve.reciprocal(RG, RG))
                link(dve.tensor_tensor(RG, RG, P_t[:, RT_G * T:(RT_G + 4) * T], ALU.mult))
                need(dve, "r_sq", l)
                for b in range(2):
                    ins = dve.tensor_tensor(RO[:, 512 * b:512 * b + 512], bankc(4 + b, 512), RG[:, 512 * b:512 * b + 512], ALU.mult)
                up(ins, "r_out")
                maxes(0)
                need(dve, "r_out", l)
                need(dve, "r_rstd", l)
                up(dve.tensor_tensor(RO, RO, RSQ, ALU.mult), "r_fin")
                for u in range(32 + 3):
                    if u == 3:
                        need(dve, "r_hi", l)
                        F = F0_t[:, M_RT * 512:(M_RT + 4) * 512].rearrange("p (k c) -> p k c", c=512)
                        up(dve.tensor_tensor(F[:, :, 256:512], RO.rearrange("p (k t) -> p k t", t=256), F[:, :, 0:256].bitcast(f32),
                                             ALU.subtract), "r_lo")
                    if u + 1 < 32:
                        maxes(u + 1)
                    if u < 32:
                        probs(u)
                    if u >= 3 and (u - 3) % 2 == 1:
                        olo((u - 3) // 2)

            def rwkv(l):
                need(dve, "o_lo", l)
                for c in range(4):
                    ins = dve.tensor_scalar(RB[:, 3072 + 256 * c:3328 + 256 * c], P[:, RW_K + c, :], vec(l, "kk", c), None, ALU.mult)
                up(ins, "w_kk")
                need(dve, "w_e", l)
                for c in range(4):
                    ins = dve.tensor_tensor_scan(PD[:, 2048 + 256 * c:2304 + 256 * c], con("scan"), RB[:, 256 * c:256 * c + 256], 0.0, ALU.mult, ALU.add)
                link(ins)
                up(dve.tensor_tensor(RB[:, 0:1024], PD[:, 2048:3072], RB[:, 0:1024], ALU.subtract), "w_scan")
                V, K, R_ = P_t[:, RW_V * T:(RW_V + 4) * T], P_t[:, RW_K * T:(RW_K + 4) * T], P_t[:, RW_R * T:(RW_R + 4) * T]
                if l:
                    dve.wait_ge(sem("vf_in"), 16)
                    link(dve.tensor_tensor(PD[:, 6144:7168], VF_t, V, ALU.subtract))
                    link(dve.tensor_tensor(PD[:, 6144:7168], PD[:, 6144:7168], RB[:, 2048:3072], ALU.mult))
                    link(dve.tensor_tensor(V, V, PD[:, 6144:7168], ALU.add))
                for c in range(4):
                    ins = dve.tensor_scalar(PD[:, 6144 + 256 * c:6400 + 256 * c], RB[:, 1024 + 256 * c:1280 + 256 * c], 1.0, vec(l, "ka", c), ALU.subtract, ALU.mult)
                link(ins)
                link(dve.scalar_tensor_tensor(out=K, in0=PD[:, 6144:7168], scalar=1.0, in1=K, op0=ALU.add, op1=ALU.mult))
                for c in range(4):
                    ins = dve.scalar_tensor_tensor(out=PD[:, 6144 + 256 * c:6400 + 256 * c], in0=P[:, RW_R + c, :], scalar=vec(l, "rk", c), in1=P[:, RW_K + c, :],
                                                   op0=ALU.mult, op1=ALU.mult)
                up(ins, "w_rk")
                need(dve, "w_kkmm", l)
                for b in range(2):
                    ins = dve.tensor_scalar(RB[:, 4096 + 512 * b:4608 + 512 * b], bankc(b, 512), 1e-24, None, ALU.max)
                up(ins, "w_kmax")
                need(dve, "w_pow", l)
                need(dve, "w_kmax", l)
                dve.tensor_copy(WC_t[:, :].rearrange("p (c k) -> p c k", k=4),
                                PD[:, 3072:4096].rearrange("p (c k t) -> p c k t", k=4, t=64)[:, :, :, 63])
                link(dve.tensor_tensor(R_, R_, PD[:, 3072:4096], ALU.mult))
                link(dve.tensor_tensor(K, K, PD[:, 4096:5120], ALU.mult))
                need(dve, "w_krs", l)
                link(dve.tensor_tensor(RB[:, 3072:4096], RB[:, 3072:4096], RB[:, 4096:5120], ALU.mult))
                link(dve.tensor_tensor(RB[:, 1024:2048], RB[:, 1024:2048], RB[:, 3072:4096], ALU.mult))
                dve.tensor_tensor(RB[:, 1024:2048], RB[:, 1024:2048], PD[:, 4096:5120], ALU.mult)
                link(dve.scalar_tensor_tensor(out=RB[:, 3072:4096], in0=RB[:, 3072:4096], scalar=-1.0, in1=PD[:, 5120:6144], op0=ALU.mult, op1=ALU.mult))
                need(dve, "w_bmm", l)
                for b in range(2):
                    ins = dve.tensor_tensor(PD[:, 1024 + 512 * b:1536 + 512 * b], bankc(2 + b, 512), V[:, 512 * b:512 * b + 512], ALU.mult)
                up(ins, "w_bv")
                up(dve.memset(ST_t[:, :], 0.0), "w_til")
                need(dve, "w_til", l)
                up(dve.memset(BD, 0.0), "w_bz")
                need(dve, "w_bz", l)
                BD5 = BD.rearrange("p (c h a t) -> p c h a t", c=4, h=2, a=2)
                for tt in range(2):
                    if tt:
                        need(dve, "w_y", l, tt)
                    for h in range(2):
                        r = slice(64 * h, 64 * h + 64)
                        for a, src in enumerate([RB[r, 3072:4096], P_t[r, RW_R * T:(RW_R + 4) * T]]):
                            s3 = src.rearrange("p (c t) -> p c t", t=T)[:, :, tt * 128:tt * 128 + 128]
                            ins = dve.tensor_copy(BD5[r, :, h, a, :], s3)
                    up(ins, "w_bd")
                    m = con("rw_mask").unsqueeze(1).to_broadcast([128, 2, 256])
                    for q in range(4):
                        need(dve, "w_l", l, 2 * tt + q // 2 + 1)
                        for x, L in enumerate([LB, LK]):
                            b = 2 * (q % 2) + x
                            ins = dve.tensor_tensor(L[:, 512 * q:512 * q + 512].rearrange("p (h w) -> p h w", w=256),
                                                    bankc((4 if q // 2 else 0) + b, 512).rearrange("p (h w) -> p h w", w=256), m, ALU.mult)
                        if q % 2:
                            up(ins, "w_lm")
                    need(dve, "w_lm", l, 2 * tt + 2)
                    LB4 = LB.rearrange("p (h a t) -> p h a t", a=2, t=128)

                    def level_mask(s, q):
                        mk = con("lev")[:, 128 * s:128 * s + 128].unsqueeze(1).to_broadcast([128, 4, 128])
                        up(dve.tensor_tensor(NM[:, 512 * q:512 * q + 512].rearrange("p (h t) -> p h t", t=128), LB4[:, 4 * q:4 * q + 4, 0, :], mk, ALU.mult), "w_nm")
                    idb = con("ident").unsqueeze(1).to_broadcast([128, 4, 128])
                    for q in range(2):
                        level_mask(0, q)
                    for q in range(2):
                        need(dve, "w_am", l, 2 * tt + q + 1)
                        dve.tensor_tensor(TA[:, 512 * q:512 * q + 512].rearrange("p (h t) -> p h t", t=128), bankc(q, 512).rearrange("p (h t) -> p h t", t=128), idb, ALU.add)
                        up(dve.tensor_tensor(TB[:, 512 * q:512 * q + 512].rearrange("p (h t) -> p h t", t=128), NM[:, 512 * q:512 * q + 512].rearrange("p (h t) -> p h t", t=128), idb, ALU.add), "w_ae")
                    for s in range(1, 6):
                        for q in range(2):
                            need(dve, "w_ae", l, 2 * tt + q + 1)
                            if s > 1:
                                need(dve, "w_pm", l, 10 * tt + 2 * (s - 2) + q + 1)
                                need(dve, "w_be", l, 10 * tt + 2 * (s - 2) + q + 1)
                            level_mask(s, q)
                        for q in range(2):
                            k = 10 * tt + 2 * (s - 1) + q + 1
                            need(dve, "w_bm", l, k)
                            if s < 5:
                                dve.tensor_tensor(TA[:, 512 * q:512 * q + 512], TA[:, 512 * q:512 * q + 512], bankc(2 + q, 512), ALU.add)
                            up(dve.tensor_tensor(TB[:, 512 * q:512 * q + 512], TB[:, 512 * q:512 * q + 512], bankc(4 + q, 512), ALU.add), "w_be")
                    need(dve, "w_be", l, 10 * tt + 10)
                    up(dve.memset(TA, 0.0), "w_xz")
                    for c in range(2):
                        ch = 2 * tt + c
                        need(dve, "w_s", l, ch + 1)
                        link(dve.tensor_tensor(SN_t[:, :], PS_t[:, 2, 0:256], ST_t[:, :], ALU.add))
                        up(dve.tensor_tensor(ST_t[:, :].rearrange("p (c i) -> p c i", i=64), SN_t[:, :].rearrange("p (c i) -> p c i", i=64),
                                             WC_t[:, :].rearrange("p (c k) -> p c k", k=4)[:, :, ch:ch + 1].to_broadcast([128, 4, 64]), ALU.mult), "w_se")
                    need(dve, "w_y", l, tt + 1)
                    Y3 = PS_t[:, 3, :].rearrange("p (h i) -> p h i", i=64)
                    YC = RB[:, 6144:6656]
                    YC3 = YC.rearrange("p (h i) -> p h i", i=64)
                    link(dve.tensor_reduce(RB[:, 7168:7176], Y3, AX.X, ALU.add))
                    link(dve.tensor_scalar(RB[:, 7168:7176], RB[:, 7168:7176], 1.0 / 64, None, ALU.mult))
                    up(dve.tensor_tensor(YC3, Y3, RB[:, 7168:7176].unsqueeze(2).to_broadcast([128, 8, 64]), ALU.subtract), "w_ysum")
                    need(dve, "w_ysq", l, tt + 1)
                    up(dve.tensor_reduce(RB[:, 7176:7184], RB[:, 6656:7168].rearrange("p (h i) -> p h i", i=64), AX.X, ALU.add), "w_yvar")
                    need(dve, "w_yrs", l, tt + 1)
                    up(dve.tensor_tensor(RB[:, 6656:7168].rearrange("p (h i) -> p h i", i=64), YC3, RB[:, 7184:7192].unsqueeze(2).to_broadcast([128, 8, 64]), ALU.mult), "w_yn")
                    need(dve, "w_yt", l, tt + 1)
                    for c in range(4):
                        ins = dve.tensor_scalar(RB[:, 6144 + 128 * c:6272 + 128 * c], PS_t[:, 4, 128 * c:128 * c + 128], vec(l, "lng", c), vec(l, "lnb", c), ALU.mult, ALU.add)
                    link(ins)
                    YO = RB[:, 6144:6656].rearrange("p (c t) -> p c t", t=128)
                    tsl = slice(tt * 128, tt * 128 + 128)
                    link(dve.tensor_tensor(YO, YO, PD[:, 1024:2048].rearrange("p (c t) -> p c t", t=T)[:, :, tsl], ALU.add))
                    up(dve.tensor_tensor(YO, YO, PD[:, 0:1024].rearrange("p (c t) -> p c t", t=T)[:, :, tsl], ALU.mult), "w_yb")
                    need(dve, "w_hi", l, tt + 1)
                    F = F0_t[:, M_RW * 512:(M_RW + 4) * 512].rearrange("p (k c) -> p k c", c=512)
                    up(dve.tensor_tensor(F[:, :, 256 + tt * 128:384 + tt * 128], YO, F[:, :, tt * 128:tt * 128 + 128].bitcast(f32), ALU.subtract), "w_lo")
                need(dve, "w_lo", l)

            dve.memset(EPS_t[:, E_RMS:E_RMS + 1], 1e-6)
            dve.memset(EPS_t[:, E_KK:E_KK + 1], 5.545177444479562)
            dve.memset(EPS_t[:, E_LN8:E_LN8 + 2], -2.0794415416798357)
            dve.memset(EPS_t[:, E_GN:E_GN + 1], 64e-5)
            dve.memset(EPS_t[:, E_LN8 + 2:E_LN8 + 3], 0.0).then_inc(const_ready, 1)
            dve.wait_ge(vec_in, 16)
            dve.wait_ge(con_in, 16)
            for n in range(KT):
                dve.wait_ge(x_hi, n + 1)
                dve.scalar_tensor_tensor(out=F0_t[:, n * 512 + 256:n * 512 + 512], in0=X_t[:, n * T:(n + 1) * T], scalar=vec(0, "g1", n),
                                         in1=F0_t[:, n * 512:n * 512 + 256].bitcast(f32), op0=ALU.mult, op1=ALU.subtract).then_inc(x_lo, 1)
                if n % 4 == 3:
                    split_lo(n // 8, 0, n // 4 % 2)
            for l in range(DEPTH):
                dve.wait_ge(rstd_ready, 2 * l + 1)
                phase(J_in(l), 4, proj_evac(NS_KC))
                phase(J_qk(l), 8, proj_evac(NS_Q), peel=0, aux=blocks(l))
                phase(J_qk(l) + 8, 4, proj_evac(NS_Q + 8))
                phase(J_cmp(l), N_CMP, cmp_evac(l), w=60)
                phase(J_rw(l), 13, proj_evac(RW_R), aux=norms(l))
                phase(J_rw(l) + 13, 4, proj_evac(RW_R + 13), peel=0, aux=gelu(l))
                for half in range(2):
                    phase(J_rt(l) + 8 * half, 8, proj_evac(RT_Q + 8 * half), peel=0, aux=shift(l, half))
                phase(J_v(l), 4, proj_evac(NS_VS), peel=0, ahead=2, aux=compress(l))
                nsa(l)
                rwkv(l)
                for s in range(2):
                    for a in range(2):
                        split_lo(J_out(l) + s, 0, a)
                phase(J_out(l), N_OUT, x_evac(2 * l + 1, l, "g2", F1_t, True))
                dve.wait_ge(rstd_ready, 2 * l + 2)
                for g in range(N_GRP):
                    phase(J_up(l, g), 16, up_evac(l, g))
                    last = g == N_GRP - 1
                    phase(J_down(l, g), 16, x_evac(2 * l + 2 if last else 0, l + 1, "g1", F0_t, last and l + 1 < DEPTH))

        @block.tensor
        def _(pe):
            def phase(J0, count, rhs, ready, base, w=T, after_first=None, peel=1, aux=None):
                def body(n, s, i):
                    slab(n, s, i, rhs, ready, base, w)
                    if n == 0 and after_first:
                        after_first()
                    if aux:
                        aux(n - peel, i)
                walk(pe, J0, count, body, peel)

            def slab(n, s, i, rhs, ready, base, w):
                    B = PS_t[:, s % RING, :]
                    for a in range(2):
                        h = 2 * s + a
                        pe.wait_ge(lo_ready, i * 8 + (h + 1))
                        if a == 0 and s >= 4:
                            pe.wait_ge(sum_ready, i * 4 + (s - 3))
                        for k8 in range(HALF):
                            k = HALF * a + k8
                            if ready and n == 0 and k in (0, 8, 14, 15):
                                pe.wait_ge(ready, base + {0: 8, 8: 14, 14: 15, 15: 16}[k])
                            c = (h % 4) * 1024 + k8 * 128
                            x = rhs(k)
                            if k == 0:
                                pe.matmul(B[:, 0:2 * w], hi_t[:, c:c + 128], x, start=True, stop=False)
                                pe.matmul(B[:, 0:w], lo_t[:, c:c + 128], x[:, 0:w], start=False, stop=False)
                            else:
                                pe.matmul(B[:, 0:w], lo_t[:, c:c + 128], x[:, 0:w], start=False, stop=False)
                                ins = pe.matmul(B[:, 0:2 * w], hi_t[:, c:c + 128], x, start=False, stop=(k == KT - 1))
                        ins.then_inc(half_done, 1)

            def stats(nm):
                def f():
                    pe.wait_ge(pool_acc, 16 * (nm + 1))
                    pe.matmul(PS_t[:, 4, 0:T], con("one_d"), acc_t[:, :], start=True, stop=True).then_inc(stat_mm, 1)
                return f

            def mm(o, a, b, start=True, stop=True):
                return pe.matmul(o, a, b, start=start, stop=stop, skip_group_check=True)

            def norms(l):
                def aux(n, i):
                    if n == 1:
                        need(pe, "n_g", l, i + 1)
                        need(pe, "n_rope", l, i + 0)
                        for b in range(2):
                            mm(bankc(4 + b, 512), con("blk_mean"), SQ[:, 512 * b:512 * b + 512])
                        Q4 = cols(P_t, i, NS_Q * T, 1024, 1024)
                        for b in range(2):
                            ins = mm(bankc(6 + b, 512), con("rot_n"), Q4[:, 512 * b:512 * b + 512])
                        up(ins, "n_mm")
                return aux

            def rotate(l):
                def aux(n, i):
                    if n == 0:
                        pe.wait_ge(evac_done, J_rt(l) + 8)
                        need(pe, "n_rope", l)
                        need(pe, "r_rope", l, i + 0)
                        R4 = cols(P_t, i, RT_Q * T, 1024, 1024)
                        for b in range(2):
                            ins = mm(bankc(4 + b, 512), con("rot_r"), R4[:, 512 * b:512 * b + 512])
                        up(ins, "r_rot")
                return aux

            def compress(l):
                def aux(n, i):
                    if n == 0:
                        need(pe, "hv_ready", l)
                        need(pe, "r_rope", l)
                        pe.wait_ge(sem("cw_in"), 16 * (l + 1))
                        for ht in range(2):
                            mm(PS_t[:, 4, 0:60], CW_t[:, 128 * ht:128 * ht + 128], HID[:, 256 + 60 * ht:316 + 60 * ht], start=ht == 0)
                        for pg in range(2):
                            for ht in range(2):
                                ins = mm(PS_t[:, 4, 256 + 64 * pg:320 + 64 * pg], HV_t[:, ht * 256 + pg * 128:ht * 256 + pg * 128 + 128],
                                         CW_t[:, 256 + 64 * ht:320 + 64 * ht], start=False)
                        up(ins, "cmp_mm")
                    if n == 1:
                        need(pe, "kc_ready", l)
                        mm(PS_t[:, 4, 64:124], con("blk_mean"), HT[:, 0:60], start=False)
                        up(mm(PS_t[:, 4, 128:188], con("rot_n"), HT[:, 64:124], start=False), "kc_mm")
                        need(pe, "w_mix", l)
                        for tt in range(2):
                            ins = pe.transpose(PS_t[:, 6, 128 * tt:128 * tt + 128], P[:, RW_X, 128 * tt:128 * tt + 128], con("ident"))
                        up(ins, "ng_t")
                    if n == 1:
                        for tt in range(2):
                            for j in range(4):
                                ins = pe.transpose(PS_t[:, 5 + 2 * tt, 128 * j:128 * j + 128], P[:, RT_V + j, 128 * tt:128 * tt + 128], con("ident"))
                        up(ins, "r_vt")
                return aux

            def nsa(l):
                need(pe, "r_vev", l)
                need(pe, "ng_e", l)
                need(pe, "kc_done", l)
                for h in range(4):
                    mm(PS_t[:, 4 + h, 0:256], P[:, RT_K + h, 0:128], P[:, RT_Q + h, :])
                    up(mm(PS_t[:, 4 + h, 256:384], P[:, RT_K + h, 128:256], P[:, RT_Q + h, 128:256], start=False), "r_in")
                pe.wait_ge(evac_done, J_out(l))
                for tt in range(2):
                    for j in range(4):
                        ins = pe.transpose(PS_t[:, 2 + tt, 128 * j:128 * j + 128], P[:, NS_VS + j, 128 * tt:128 * tt + 128], con("ident"))
                up(ins, "nv_t")
                for tt in range(2):
                    for qt in range(8):
                        ins = mm(PS_t[:, tt, 32 * qt:32 * qt + 32], P[:, NS_Q + qt, 128 * tt:128 * tt + 128], KTC_t[:, 32 * (qt // 4):32 * (qt // 4) + 32], start=qt == 0)
                    up(ins, "cs_mm")
                for h in range(4):
                    need(pe, "r_dec", l, h + 1 if h > 1 else 2)
                    O = PS_t[:, 4 + h // 2, 256 * (h % 2):256 * (h % 2) + 256]
                    mm(O, P_t[:, RT_V * T + 128 * h:RT_V * T + 128 * h + 128], INN[:, 384 * h:384 * h + 256], start=h % 2 == 0, stop=False)
                    ins = mm(O[:, 128:256], P_t[:, RT_V * T + 512 + 128 * h:RT_V * T + 640 + 128 * h], INN[:, 384 * h + 256:384 * h + 384], start=False)
                up(ins, "r_o")
                need(pe, "nv_ev", l)
                for tt in range(2):
                    need(pe, "cs_p", l, tt + 1)
                    for j in range(2):
                        ins = pe.transpose(PS_t[:, 6 + tt, 128 * j:128 * j + 128], CS[:, 256 * tt + 128 * j:256 * tt + 128 * j + 128], con("ident"))
                    up(ins, "cs_t")
                need(pe, "r_sq", l)
                for b in range(2):
                    ins = mm(bankc(2 + b, 512), con("one_h"), RSQ[:, 512 * b:512 * b + 512])
                up(ins, "r_mm")
                need(pe, "cs_ev", l)

                def scores(u):
                    qt, tt, br = UN[u]
                    w = 128 * (tt + 1)
                    if u >= 2:
                        need(pe, "s_max", l, u - 1)
                    for h in range(2):
                        r = slice(64 * h, 64 * h + 64)
                        ins = mm(PS_t[:, u % 2 + 6 * h, 0:w], P[r, NS_Q + qt, 128 * tt:128 * tt + 128],
                                 P[r, NS_KS + 2 * br + qt // 4, 0:w])
                    up(ins, "s_mm")

                def transposes(u):
                    qt, tt, br = UN[u]
                    w = 128 * (tt + 1)
                    need(pe, "s_p", l, u + 1)
                    if u == 0:
                        need(pe, "r_rstd", l)
                    if u >= 2:
                        need(pe, "p_ev", l, u - 1)
                    S = SB(u)
                    for j in range(2 * (tt + 1)):
                        ins = pe.transpose(PS_t[:, 2 + u % 2, 128 * j:128 * j + 128], S[:, 128 * j:128 * j + 128], con("ident"))
                    up(ins, "p_t")

                def values(u):
                    qt, tt, br = UN[u]
                    v = u // 2
                    need(pe, "p_ev", l, u + 1)
                    O = PS_t[:, 4 + v % 2, 0:128]
                    if u % 2 == 0:
                        if v == 0:
                            need(pe, "nz", l)
                            need(pe, "r_out", l)
                        if v >= 2:
                            need(pe, "o_lo", l, v - 1)
                        mm(O, RA[:, 512 + 512 * (qt // 4) + 128 * (qt % 4):640 + 512 * (qt // 4) + 128 * (qt % 4)],
                           PC[:, 256 * tt + 128 * (qt // 4):256 * tt + 128 * (qt // 4) + 128], start=True, stop=False)
                    for h in range(2):
                        g = 2 * (qt // 4) + h
                        for kt in range(tt + 1):
                            V = P_t[:, NS_VS * T + 512 * kt + 256 * br + 64 * g:NS_VS * T + 512 * kt + 256 * br + 64 * g + 64]
                            ins = mm(O[64 * h:64 * h + 64, :], V, PTB[:, 512 * (u % 2) + 128 * (h * (tt + 1) + kt):512 * (u % 2) + 128 * (h * (tt + 1) + kt) + 128],
                                     start=False, stop=u % 2 == 1)
                    if u % 2:
                        up(ins, "o_mm")
                    else:
                        up(ins, "o_half")

                scores(0)
                scores(1)
                for u in range(32 + 1):
                    if u + 2 < 32:
                        scores(u + 2)
                    if u < 32:
                        transposes(u)
                    if u >= 1:
                        values(u - 1)

            def rwkv(l):
                pe.wait_ge(sem("small_in"), 16 * (l + 1))
                need(pe, "o_lo", l)
                need(pe, "w_tw", l)
                w2, a2, v2 = (LW_t[:, LW[n][0]:LW[n][1]] for n in ("w2", "a2", "v2"))
                for b, (w, src) in enumerate([(w2, RW_W), (a2, RW_A), (v2, RW_X)][:3 if l else 2]):
                    for c in range(4):
                        mm(PS_t[:, 2 * b + c // 2, (c % 2) * 256:(c % 2) * 256 + 256], w[:, 128 * c:128 * c + 128], P[:, src, :], start=c % 2 == 0)
                need(pe, "w_xg", l)
                for c in range(4):
                    for k in range(2):
                        g2 = LW_t[:, LW["g2"][0] + 512 * k + 128 * c:LW["g2"][0] + 512 * k + 128 * c + 128]
                        ins = mm(PS_t[:, 6 + c // 2, (c % 2) * 256:(c % 2) * 256 + 256], g2, P[:, RW_G + k, :], start=c % 2 == 0 and k == 0, stop=k == 1)
                up(ins, "w_lr")
                need(pe, "w_kk2", l)
                need(pe, "w_e", l)
                for b in range(2):
                    ins = mm(bankc(b, 512), con("blk_sum"), RB[:, 4096 + 512 * b:4608 + 512 * b])
                up(ins, "w_kkmm")
                need(pe, "w_rk", l)
                for b in range(2):
                    ins = mm(bankc(2 + b, 512), con("blk_sum"), PD[:, 6144 + 512 * b:6656 + 512 * b])
                up(ins, "w_bmm")
                need(pe, "w_til", l)
                for tt in range(2):
                    for c in range(4):
                        ins = pe.transpose(PS_t[:, tt, 128 * c:128 * c + 128], P[:, RW_V + c, 128 * tt:128 * tt + 128], con("ident"))
                up(ins, "w_vt")
                VT = P_t[:, RW_W * T:RW_W * T + 1024]
                BT = P_t[:, RW_V * T:RW_V * T + 512]
                KTt = P_t[:, RW_V * T + 512:RW_V * T + 1024]
                for tt in range(2):
                    ts_ = slice(128 * tt, 128 * tt + 128)
                    need(pe, "w_vev", l)
                    if tt:
                        need(pe, "w_se", l, 2 * tt)
                        need(pe, "w_ysum", l, tt)
                    for c in range(4):
                        pe.transpose(PS_t[:, 2, 128 * c:128 * c + 128], RB[:, 1024 + 256 * c + 128 * tt:1152 + 256 * c + 128 * tt], con("ident"))
                        ins = pe.transpose(PS_t[:, 3, 128 * c:128 * c + 128], P[:, RW_K + c, ts_], con("ident"))
                    up(ins, "w_bkt")
                    need(pe, "w_bd", l, tt + 1)
                    need(pe, "w_bkev", l, tt + 1)
                    if tt:
                        need(pe, "w_yb", l, tt)
                    for c in range(4):
                        rhs = BD[:, 512 * c:512 * c + 512]
                        b0 = (4 if c // 2 else 0) + 2 * (c % 2)
                        mm(bankc(b0, 512), RB[:, 1024 + 256 * c + 128 * tt:1152 + 256 * c + 128 * tt], rhs)
                        ins = mm(bankc(b0 + 1, 512), P[:, RW_K + c, ts_], rhs)
                        if c % 2:
                            up(ins, "w_l")
                    need(pe, "w_lm", l, 2 * tt + 2)
                    for q in range(2):
                        need(pe, "w_nm", l, 12 * tt + q + 1)
                        for h in range(4):
                            o = 512 * q + 128 * h
                            ins = mm(PS_t[:, q, 128 * h:128 * h + 128], NM[:, o:o + 128], con("ident"), start=h == 0)
                        up(ins, "w_am")
                    for s in range(1, 6):
                        for q in range(2):
                            need(pe, "w_nm", l, 12 * tt + 2 * s + q + 1)
                            if s == 1:
                                need(pe, "w_ae", l, 2 * tt + q + 1)
                            else:
                                need(pe, "w_be", l, 10 * tt + 2 * (s - 2) + q + 1)
                            for h in range(4):
                                o = 512 * q + 128 * h
                                ins = mm(PS_t[:, q, 128 * h:128 * h + 128], NM[:, o:o + 128], TA[:, o:o + 128], start=h == 0)
                            up(ins, "w_pm")
                        for q in range(2):
                            k = 10 * tt + 2 * (s - 1) + q + 1
                            need(pe, "w_pe", l, k)
                            for h in range(4):
                                o = 512 * q + 128 * h
                                if s < 5:
                                    mm(PS_t[:, 2 + q, 128 * h:128 * h + 128], TB[:, o:o + 128], PP[:, o:o + 128], start=h == 0)
                                ins = mm(PS_t[:, 4 + q, 128 * h:128 * h + 128], PP[:, o:o + 128], TB[:, o:o + 128], start=h == 0)
                            up(ins, "w_bm")
                    need(pe, "w_xz", l, tt + 1)
                    BD5 = BD.rearrange("p (c h a t) -> p c h a t", c=4, h=2, a=2)
                    LB4 = LB.rearrange("p (h a t) -> p h a t", a=2, t=128)
                    LK4 = LK.rearrange("p (h a t) -> p h a t", a=2, t=128)
                    Y = PS_t[:, 3, :]
                    for h in range(8):
                        mm(Y[:, 64 * h:64 * h + 64], LK4[:, h, 1, :], VT[:, 512 * tt + 64 * h:512 * tt + 64 * h + 64], start=h == 0, stop=False)
                    for c in range(2):
                        ch = 2 * tt + c
                        r = slice(64 * c, 64 * c + 64)
                        if ch:
                            need(pe, "w_se", l, ch)
                        for h in range(8):
                            o = slice(64 * h, 64 * h + 64)
                            S = ST_t[:, 64 * (h // 2):64 * (h // 2) + 64]
                            mm(PS_t[r, 0, o], BD5[:, h // 2, h % 2, 0, r], S, start=h == 0, stop=False)
                            ins = mm(PS_t[r, 0, o], LK4[:, h, 0, r], VT[:, 512 * tt + 64 * h:512 * tt + 64 * h + 64], start=False)
                        up(ins, "w_x")
                        for h in range(8):
                            mm(Y[r, 64 * h:64 * h + 64], BD5[:, h // 2, h % 2, 1, r], ST_t[:, 64 * (h // 2):64 * (h // 2) + 64], start=False, stop=False)
                        need(pe, "w_xe", l, ch + 1)
                        for h in range(8):
                            ins = mm(PS_t[r, 1, 64 * h:64 * h + 64], TB[:, 128 * h + 64 * c:128 * h + 64 * c + 64], TA[:, 64 * h:64 * h + 64], start=h == 0)
                        up(ins, "w_u")
                        need(pe, "w_ue", l, ch + 1)
                        for h in range(8):
                            o = PS_t[64 * (h % 2):64 * (h % 2) + 64, 2, 64 * (h // 2):64 * (h // 2) + 64]
                            hs = slice(64 * h, 64 * h + 64)
                            mm(o, BT[r, hs], TA[r, 512 + 64 * h:576 + 64 * h], start=h < 2, stop=False)
                            ins = mm(o, KTt[r, hs], VT[r, 512 * tt + 64 * h:512 * tt + 64 * h + 64], start=False)
                        up(ins, "w_s")
                    for h in range(8):
                        ins = mm(Y[:, 64 * h:64 * h + 64], LB4[:, h, 1, :], TA[:, 512 + 64 * h:576 + 64 * h], start=False)
                    up(ins, "w_y")
                    need(pe, "w_yn", l, tt + 1)
                    for c in range(4):
                        ins = pe.transpose(PS_t[:, 4, 128 * c:128 * c + 128], RB[:, 6656 + 128 * c:6784 + 128 * c], con("ident"))
                    up(ins, "w_yt")

            pe.wait_ge(con_in, 16)
            for l in range(DEPTH):
                def F0(k):
                    return F0_t[:, 512 * k:512 * k + 512]
                phase(J_in(l), 4, F0, x_lo if l == 0 else evac_done, J_down(l - 1, N_GRP - 1) if l else 0, after_first=stats(2 * l))
                phase(J_qk(l), 12, F0, None, 0)
                for kv in range(2):
                    def blk(k, kv=kv):
                        return BLK_t[:, 1920 * kv + 120 * k:1920 * kv + 120 * k + 120]
                    need(pe, "blk_lo", l, kv + 1)
                    for n in range(2):
                        slab(n, J_cmp(l) + 2 * kv + n, 0, blk, None, 0, 60)
                phase(J_rw(l), 13, F0, None, 0, aux=norms(l))
                phase(J_rw(l) + 13, 12, F0, None, 0, peel=0)
                phase(J_rt(l) + 8, 8, F0, None, 0, peel=0, aux=rotate(l))
                phase(J_v(l), 4, F0, None, 0, peel=0, aux=compress(l))
                nsa(l)
                rwkv(l)
                need(pe, "w_lo", l)
                phase(J_out(l), N_OUT, lambda k: F0_t[:, 512 * k:512 * k + 512], None, 0)
                for g in range(N_GRP):
                    phase(J_up(l, g), 16, lambda k: F1_t[:, 512 * k:512 * k + 512], evac_done, J_out(l), after_first=stats(2 * l + 1) if g == 0 else None)
                    phase(J_down(l, g), 16, lambda k: U_t[:, 512 * k:512 * k + 512], evac_done, J_up(l, g))


def _pad(a, n):
    import numpy as np
    return np.concatenate([a, np.zeros(a.shape[:-1] + (n - a.shape[-1],), a.dtype)], -1)


def _constants():
    import numpy as np
    p = np.arange(128)
    c = {}
    c["ident"] = np.eye(128)
    c["one_d"] = np.full((128, 128), 1.0 / D)
    c["blk_sum"] = (p[:, None] // 64 == p[None, :] // 64).astype(float)
    c["blk_mean"] = c["blk_sum"] / 64
    c["one_h"] = np.full((128, 128), 1.0 / 128)

    def rot(h):
        m = np.zeros((128, 128))
        for j in range(128):
            if j % (2 * h) < h:
                m[j + h, j] = -1
            else:
                m[j - h, j] = 1
        return m

    def trig(h, pos):
        f = (np.float32(10000.0) ** (-np.arange(h, dtype=np.float32) / np.float32(h))).astype(np.float32)
        a = (pos.astype(np.float32)[None, :] * f[p % h][:, None]).astype(np.float32).astype(np.float64)
        return np.cos(a), np.sin(a)
    c["rot_r"], c["rot_n"] = rot(64), rot(32)
    t = np.arange(T)
    c["cos_r"], c["sin_r"] = trig(64, t)
    c["cos_n"], c["sin_n"] = trig(32, t)
    c["cos_c"], c["sin_c"] = trig(32, np.arange(16) * 16 + 31)
    lag = t[None, :] - p[:, None]
    c["decay"] = np.concatenate([np.where(lag >= 0, (1 - 2.0 ** (-5 - h)) ** np.maximum(lag, 0), 0.0) for h in range(4)], 1) * 128 ** -0.5
    c["causal"] = np.concatenate([np.zeros((128, 128)), np.where(p[None, :] <= p[:, None], 0.0, -1e30)], 1)
    n = np.arange(16)
    vis = np.concatenate([(16 * n[None, :] + 31 <= tt * 128 + p[:, None]) & (n[None, :] < 15) for tt in range(2)], 1)
    c["cmp_add"], c["cmp_vis"] = np.where(vis, 0.0, -1e30), vis.astype(float)
    same = p[:, None] // 64 == p[None, :] // 64
    c["rw_mask"] = np.concatenate([same & (p[:, None] < p[None, :]), same & (p[:, None] <= p[None, :])], 1).astype(float)
    c["lev"] = np.concatenate([((p[None, :] >> s) % 2 == 1) & ((p[:, None] >> s) == (p[None, :] >> s) - 1) for s in range(6)], 1).astype(float)
    c["scan"] = np.broadcast_to((t % 64 != 0).astype(float), (128, T))
    c["vcz"] = np.stack([(p // 32 == s // 2) & (p % 32 // 16 == s % 2) for s in range(8)], 1).astype(float)
    return np.concatenate([np.asarray(c[k], np.float32) for k in CON], 1)


def kernel(**inputs):
    import numpy as np
    import concourse.bacc as bacc
    from concourse.bass_utils import run_bass_kernel_spmd as run

    a = {k: np.asarray(v) for k, v in inputs.items()}
    heads = [8 * pg + 4 * h + q for pg in range(2) for q in range(4) for h in range(2)]
    hcols = np.concatenate([np.arange(64) + 64 * h for h in heads])

    def tiles(w):
        return w.reshape(16, 128, -1, 128).transpose(2, 1, 0, 3).reshape(-1, 128, 2048)

    slabs = np.empty((SLABS, 128, 2048), np.float32)
    vecs, small, cmpw = [], [], []
    o_rw, o_ns = 2048, 2048 + 1984

    def cols(v):
        return v.reshape(-1, 128).T

    for l in range(DEPTH):
        w = a["w_in"][l]
        vres = a["w_in_vres"][l - 1] if l else np.zeros((D, 64), np.float32)
        rw, ns = w[:, o_rw:o_ns], w[:, o_ns:]
        kv = [ns[:, 1024 + 256 * i:1280 + 256 * i] for i in range(6)]
        gates = ns[:, 2560:2608].reshape(D, 16, 3)[:, heads].reshape(D, 48)
        shared = [rw[:, 0:1536], _pad(rw[:, 1536:1632], 128), _pad(rw[:, 1632:1728], 128), rw[:, 1728:1984],
                  _pad(np.concatenate([vres, gates], 1), 128), w[:, 0:2048], kv[3], kv[5]]
        j = l * LAYER_SLABS
        slabs[j:j + 16] = tiles(np.concatenate([kv[0], kv[1], ns[:, hcols], kv[2], kv[4]], 1))
        j += 16
        slabs[j:j + 2] = tiles(a["nsa_cmp_k_w1"][l])
        slabs[j + 2:j + 4] = tiles(a["nsa_cmp_v_w1"][l])
        j += N_CMP
        slabs[j:j + N_IN - 16] = tiles(np.concatenate(shared, 1))
        j += N_IN - 16
        wo = a["w_out"][l]
        slabs[j:j + N_OUT] = tiles(np.concatenate([wo[512:1024], wo[0:512], wo[1024:][hcols]]))
        j += N_OUT
        for g in range(N_GRP):
            slabs[j:j + 16] = tiles(a["w_up"][l][:, 2048 * g:2048 * g + 2048])
            slabs[j + 16:j + 32] = tiles(a["w_down"][l][2048 * g:2048 * g + 2048])
            j += 32
        mix = a["rwkv_mix"][l]
        vmix = a["rwkv_vres_mix"][l - 1] if l else np.zeros(64, np.float32)
        v0 = a["rwkv_v0"][l - 1] if l else np.zeros(512, np.float32)
        v2 = a["rwkv_v2"][l - 1] if l else np.zeros((64, 512), np.float32)
        mixes = np.concatenate([mix[0:1536], _pad(mix[1536:1632], 128), _pad(mix[1632:1728], 128), mix[1728:1984], _pad(vmix, 128)])

        def dup(v):
            return np.concatenate([v, v])[:, None]

        def rows(w):
            return _pad(w.T, 128).T

        kn = a["nsa_k_norm"][l]
        pe = [a["nsa_cmp_pe"][l, i].reshape(16, 128).T for i in range(2)]
        vecs.append(np.concatenate([cols(a["ln1_g"][l]), cols(a["ln2_g"][l]), cols(mixes), cols(a["rwkv_w0"][l]), cols(a["rwkv_a0"][l]),
                                    cols(v0), cols(a["rwkv_k_k"][l]), cols(a["rwkv_k_a"][l]), cols(a["rwkv_r_k"][l].reshape(-1)),
                                    cols(a["rwkv_ln_g"][l]), cols(a["rwkv_ln_b"][l]), dup(kn[0]), *[dup(a["nsa_q_norm"][l])] * 4, dup(kn[1]), dup(kn[2]),
                                    pe[0], pe[1]], 1))
        g2 = a["rwkv_g2"][l]
        small.append(np.concatenate([rows(a["rwkv_w2"][l]), rows(a["rwkv_a2"][l]), rows(v2), g2[0:128], g2[128:256]], 1))
        k2, w2 = a["nsa_cmp_k_w2"][l], a["nsa_cmp_v_w2"][l]
        cmpw.append(np.concatenate([k2[0:128], k2[0:128], k2[128:256], k2[128:256], w2[0:128], w2[128:256]], 1))

    x = np.ascontiguousarray(a["x"].reshape(T, 16, 128).transpose(2, 1, 0).reshape(128, 16 * T))
    arrays = {"slabs": slabs, "x": x, "vecs": np.ascontiguousarray(np.concatenate(vecs, 1)), "consts": np.ascontiguousarray(_constants()),
              "small": np.ascontiguousarray(np.stack(small)), "cmpw": np.ascontiguousarray(np.stack(cmpw))}
    nc = bacc.Bacc("TRN2", target_bir_lowering=False, num_devices=1)
    f32 = mybir.dt.float32
    args = [nc.dram_tensor(f"in_{k}", v.shape, f32, kind="ExternalInput").ap() for k, v in arrays.items()]
    out = nc.dram_tensor("out_t", (128, 16 * T), f32, kind="ExternalOutput").ap()
    v_first = nc.dram_tensor("v_first", (128, 4 * T), f32, kind="Internal").ap()
    hybrid_trunk(nc, *args, out, v_first)
    r = run(nc, [{f"in_{k}": v for k, v in arrays.items()}], core_ids=[0])
    got = np.asarray(r.results[0]["out_t"])
    return got.reshape(128, 16, T).transpose(2, 1, 0).reshape(1, T, D)
```
